# Optimizing a Trainium2 kernel written in Bass

```python
import math
import jax, jax.numpy as jnp
from jax import lax
import numpy as np

D_MODEL = 1024
BATCH = 1
SEQ = 512
DEPTH = 2

HEAD_DIM = 64
N_Q_HEADS = 16
N_KV_HEADS = 4
Q_PER_KV = N_Q_HEADS // N_KV_HEADS
WINDOW = 128
BLOCK = 128
ROPE_THETA = 10000.0
ATTN_Q_W = N_Q_HEADS * HEAD_DIM
ATTN_KV_W = N_KV_HEADS * HEAD_DIM
CONV_DIM = D_MODEL
CONV_WIDTH = 31
IN_COLS = ATTN_Q_W + 2 * ATTN_KV_W + 2 * CONV_DIM + 2 * D_MODEL
N_KEYS = 128
N_EXPERTS = N_KEYS * N_KEYS
N_RET_HEADS = 8
D_KEY = 256
HALF_KEY = D_KEY // 2
TOPK_HALF = 16
TOPK = 16
PEER_CHUNK = 128
EPS = 1e-6
NEG_INF = -1e30

kernel_name = "hybrid_swa_conformer_peer_adaln"

def rms_norm(x, g):
    xf = x.astype(jnp.float32)
    y = xf * lax.rsqrt(jnp.mean(xf * xf, axis=-1, keepdims=True) + EPS)
    return (y * g.astype(jnp.float32)).astype(x.dtype)

def layer_norm(x, g, b):
    xf = x.astype(jnp.float32)
    mu = jnp.mean(xf, axis=-1, keepdims=True)
    var = jnp.mean(jnp.square(xf - mu), axis=-1, keepdims=True)
    y = (xf - mu) * lax.rsqrt(var + EPS)
    return (y * g.astype(jnp.float32) + b.astype(jnp.float32)).astype(x.dtype)

def rope_tables(positions):
    inv = ROPE_THETA ** (-jnp.arange(0, HEAD_DIM, 2, dtype=jnp.float32) / HEAD_DIM)
    ang = positions.astype(jnp.float32)[..., None] * inv
    return jnp.cos(ang)[:, :, None, :], jnp.sin(ang)[:, :, None, :]

def apply_rope(t, cos, sin):
    t1, t2 = jnp.split(t.astype(jnp.float32), 2, axis=-1)
    return jnp.concatenate([t1 * cos - t2 * sin, t2 * cos + t1 * sin], axis=-1).astype(t.dtype)

def sliding_window_attention(q, k, v, sinks):
    B, S = q.shape[0], q.shape[1]
    nb = S // BLOCK
    qb = q.reshape(B, nb, BLOCK, N_KV_HEADS, Q_PER_KV, HEAD_DIM)

    def band(t):
        tb = t.reshape(B, nb, BLOCK, N_KV_HEADS, HEAD_DIM)
        prev = jnp.concatenate([jnp.zeros_like(tb[:, :1]), tb[:, :-1]], axis=1)
        return jnp.concatenate([prev, tb], axis=2)

    kb, vb = band(k), band(v)
    s = jnp.einsum('bnqgrd,bnkgd->bngrqk', qb, kb).astype(jnp.float32) * (HEAD_DIM ** -0.5)
    qi = jnp.arange(BLOCK)[:, None]
    kj = jnp.arange(2 * BLOCK)[None, :]
    diff = qi + BLOCK - kj
    in_window = (diff >= 0) & (diff < WINDOW)
    key_abs = jnp.arange(nb)[:, None, None] * BLOCK + kj[None] - BLOCK
    mask = in_window[None] & (key_abs >= 0)
    s = jnp.where(mask[None, :, None, None], s, NEG_INF)
    sink = sinks.astype(jnp.float32).reshape(N_KV_HEADS, Q_PER_KV)[None, None, :, :, None, None]
    m = jnp.maximum(jnp.max(s, axis=-1, keepdims=True), sink)
    p = jnp.exp(s - m)
    p = p / (jnp.sum(p, axis=-1, keepdims=True) + jnp.exp(sink - m))
    o = jnp.einsum('bngrqk,bnkgd->bnqgrd', p.astype(vb.dtype), vb)
    return o.reshape(B, S, N_Q_HEADS * HEAD_DIM)

def causal_depthwise_conv(u, w, b):
    y = lax.conv_general_dilated(u, w[:, None, :].astype(u.dtype), window_strides=(1,),
                                 padding=[(CONV_WIDTH - 1, 0)],
                                 dimension_numbers=('NWC', 'WIO', 'NWC'),
                                 feature_group_count=u.shape[-1])
    return y + b.astype(u.dtype)

def hybrid_mixer(h, cos, sin, w_in, q_norm_g, k_norm_g, sinks, w_o_attn,
                 conv_w, conv_b, conv_ln_g, conv_ln_b, w_o_conv, w_out):
    B, S, _ = h.shape
    z = h @ w_in
    cuts = [ATTN_Q_W, ATTN_Q_W + ATTN_KV_W, ATTN_Q_W + 2 * ATTN_KV_W,
            ATTN_Q_W + 2 * ATTN_KV_W + 2 * CONV_DIM]
    q, k, v, glu, gates = jnp.split(z, cuts, axis=-1)
    q = apply_rope(rms_norm(q.reshape(B, S, N_Q_HEADS, HEAD_DIM), q_norm_g), cos, sin)
    k = apply_rope(rms_norm(k.reshape(B, S, N_KV_HEADS, HEAD_DIM), k_norm_g), cos, sin)
    v = v.reshape(B, S, N_KV_HEADS, HEAD_DIM)
    attn = sliding_window_attention(q, k, v, sinks) @ w_o_attn
    ga, gb = jnp.split(glu, 2, axis=-1)
    u = ga * jax.nn.sigmoid(gb)
    u = causal_depthwise_conv(u, conv_w, conv_b)
    u = jax.nn.silu(layer_norm(u, conv_ln_g, conv_ln_b))
    conv = u @ w_o_conv
    g_attn, g_conv = jnp.split(gates, 2, axis=-1)
    merged = jax.nn.sigmoid(g_attn) * attn + jax.nn.sigmoid(g_conv) * conv
    return merged @ w_out

def peer(h, w_query, sub_keys, u_tab, v_tab):
    B, S, D = h.shape
    T = B * S
    xt = h.reshape(T, D)
    q = (xt @ w_query).reshape(T, N_RET_HEADS, 2, HALF_KEY)
    s = jnp.einsum('thpd,hpnd->thpn', q, sub_keys).astype(jnp.float32)
    s_half, i_half = lax.top_k(s, TOPK_HALF)
    cand_s = (s_half[:, :, 0, :, None] + s_half[:, :, 1, None, :]).reshape(T, N_RET_HEADS, TOPK_HALF * TOPK_HALF)
    cand_i = (i_half[:, :, 0, :, None] * N_KEYS + i_half[:, :, 1, None, :]).reshape(T, N_RET_HEADS, TOPK_HALF * TOPK_HALF)
    top_s, pos = lax.top_k(cand_s, TOPK)
    ids = jnp.take_along_axis(cand_i, pos, axis=-1)
    gates = jax.nn.softmax(top_s, axis=-1)

    def chunk(args):
        xc, idc, gc = args
        a = jax.nn.gelu(jnp.einsum('chkd,cd->chk', u_tab[idc], xc).astype(jnp.float32), approximate=False)
        coef = (gc * a).astype(xc.dtype)
        return jnp.einsum('chk,chkd->cd', coef, v_tab[idc])

    nc = T // PEER_CHUNK
    y = lax.map(chunk, (xt.reshape(nc, PEER_CHUNK, D),
                        ids.reshape(nc, PEER_CHUNK, N_RET_HEADS, TOPK),
                        gates.reshape(nc, PEER_CHUNK, N_RET_HEADS, TOPK)))
    return y.reshape(B, S, D)

def setup_inputs(seed: int = 0) -> dict:
    key = jax.random.key(seed)
    ks = jax.random.split(key, 24)
    f32 = jnp.float32
    D = D_MODEL

    def nrm(k, shape, scale):
        return jax.random.normal(k, shape, f32) * scale

    x = jax.random.normal(ks[0], (BATCH, SEQ, D), f32)
    c = jax.random.normal(ks[1], (BATCH, D), f32)
    offset = jax.random.randint(ks[2], (BATCH, 1), 0, 1024, dtype=jnp.int32)
    positions = (jnp.arange(SEQ, dtype=jnp.int32)[None, :] + offset).astype(jnp.int32)
    return {
        "x": x,
        "c": c,
        "positions": positions,
        "ada_w": nrm(ks[3], (DEPTH, D, 6 * D), 0.5 * D ** -0.5),
        "ada_b": nrm(ks[4], (DEPTH, 6 * D), 0.01),
        "norm_mix_g": 1.0 + nrm(ks[5], (DEPTH, D), 0.05),
        "w_in": nrm(ks[6], (DEPTH, D, IN_COLS), D ** -0.5),
        "q_norm_g": 1.0 + nrm(ks[7], (DEPTH, HEAD_DIM), 0.05),
        "k_norm_g": 1.0 + nrm(ks[8], (DEPTH, HEAD_DIM), 0.05),
        "attn_sinks": nrm(ks[9], (DEPTH, N_Q_HEADS), 0.5),
        "w_o_attn": nrm(ks[10], (DEPTH, ATTN_Q_W, D), ATTN_Q_W ** -0.5),
        "conv_w": nrm(ks[11], (DEPTH, CONV_WIDTH, CONV_DIM), CONV_WIDTH ** -0.5),
        "conv_b": nrm(ks[12], (DEPTH, CONV_DIM), 0.01),
        "conv_ln_g": 1.0 + nrm(ks[13], (DEPTH, CONV_DIM), 0.05),
        "conv_ln_b": nrm(ks[14], (DEPTH, CONV_DIM), 0.01),
        "w_o_conv": nrm(ks[15], (DEPTH, CONV_DIM, D), CONV_DIM ** -0.5),
        "w_out": nrm(ks[16], (DEPTH, D, D), D ** -0.5),
        "norm_ffn_g": 1.0 + nrm(ks[17], (DEPTH, D), 0.05),
        "peer_w_query": nrm(ks[18], (DEPTH, D, N_RET_HEADS * D_KEY), D ** -0.5),
        "peer_sub_keys": nrm(ks[19], (DEPTH, N_RET_HEADS, 2, N_KEYS, HALF_KEY), HALF_KEY ** -0.5),
        "peer_u": nrm(ks[20], (DEPTH, N_EXPERTS, D), D ** -0.5),
        "peer_v": nrm(ks[21], (DEPTH, N_EXPERTS, D), 0.5),
    }

def reference(x, c, positions, ada_w, ada_b, norm_mix_g, w_in, q_norm_g, k_norm_g, attn_sinks,
              w_o_attn, conv_w, conv_b, conv_ln_g, conv_ln_b, w_o_conv, w_out, norm_ffn_g,
              peer_w_query, peer_sub_keys, peer_u, peer_v):
    cos, sin = rope_tables(positions)
    c_act = jax.nn.silu(c)
    for l in range(DEPTH):
        mod = c_act @ ada_w[l] + ada_b[l]
        sh1, sc1, g1, sh2, sc2, g2 = [m[:, None, :] for m in jnp.split(mod, 6, axis=-1)]
        h = rms_norm(x, norm_mix_g[l]) * (1.0 + sc1) + sh1
        x = x + g1 * hybrid_mixer(h, cos, sin, w_in[l], q_norm_g[l], k_norm_g[l], attn_sinks[l],
                                  w_o_attn[l], conv_w[l], conv_b[l], conv_ln_g[l], conv_ln_b[l],
                                  w_o_conv[l], w_out[l])
        h = rms_norm(x, norm_ffn_g[l]) * (1.0 + sc2) + sh2
        x = x + g2 * peer(h, peer_w_query[l], peer_sub_keys[l], peer_u[l], peer_v[l])
    return x


_drawn_inputs = setup_inputs


def setup_inputs(seed=0):
    import zlib

    import numpy as np

    out = dict(_drawn_inputs(seed))
    spreads = {}
    factors = {'ada_b': 3.225,
     'norm_mix_g': 3.809,
     'q_norm_g': 8.0,
     'k_norm_g': 8.0,
     'attn_sinks': 8.0,
     'conv_b': 8.0,
     'conv_ln_g': 3.986,
     'conv_ln_b': 8.0}
    for name, (base, spread) in spreads.items():
        noise = np.random.default_rng([zlib.crc32(name.encode()), seed]).standard_normal(out[name].shape)
        drawn = base * np.exp(spread * noise) if base else spread * noise
        out[name] = __import__('jax').numpy.asarray(drawn.astype(out[name].dtype))
    for name, factor in factors.items():
        out[name] = (out[name] * factor).astype(out[name].dtype)
    return out
```

```python
from contextlib import ExitStack

import numpy as np
import concourse.bass as bass
from concourse import mybir

F32 = mybir.dt.float32
F32R = mybir.dt.float32r
U32 = mybir.dt.uint32
I32 = mybir.dt.int32
ALU = mybir.AluOpType
ACT = mybir.ActivationFunctionType
AX = mybir.AxisListType.X

P = 128
DEPTH, D, T = 2, 1024, 512
C = D // P
HEAD, NKV, R = 64, 4, 4
NB = T // P
TAPS = 31
PAD = TAPS - 1
NKEYS = 128
RH, TOPK = 8, 16
EPS = 1e-6
LOWEST = -3.0e38
GLU_LATE = 2 * C - 2
EARLY = C // 2
EARLY_TAPS = -(-EARLY * TAPS // (NB * NKV - 2))
LN_STEPS = 2 * C + 3
TOP_STEPS = 145

I_Q, I_K, I_V = 0, 8, 10
I_GLU = 12
I_AG = 28
I_CG = 44
I_OUT = 60
I_QRY = 68
I_U = 84
I_W = I_U + NKEYS
NT = I_W + NKEYS
NE = I_W

O_GN = 0
O_CW = O_GN + 2 * C
O_CB = O_CW + C * TAPS
O_LG = O_CB + C
O_LB = O_LG + C
O_QG = O_LB + C
O_KG = O_QG + 1
O_SK = O_KG + 1
O_AB = O_SK + NKV * R
PL = O_AB + 6 * C

K_ID, K_ONE, K_BLK, K_PERM, K_IOTA, K_M0, K_M1, K_INV = 0, 128, 256, 384, 512, 640, 896, 1152
NCON = 1153

MAGIC = 12582912.0
PI = float(np.float32(3.1415925))
TP1 = 6.28125
TP2 = float(np.float32(0.00193500518798828125))
TP3 = float(2 * np.pi - TP1 - TP2)


def constants():
    k = np.arange(P)
    con = np.zeros((P, NCON), np.float32)
    con[:, K_ID:K_ID + P] = np.eye(P)
    con[:, K_ONE:K_ONE + P] = 1.0
    con[:, K_BLK:K_BLK + P] = (k[:, None] // HEAD == k[None] // HEAD)
    half = HEAD // 2
    for m in range(P):
        if m % HEAD < half:
            con[m + half, K_PERM + m] = -1.0
        else:
            con[m - half, K_PERM + m] = 1.0
    con[:, K_IOTA:K_IOTA + P] = k[None]
    diff = k[:, None] + P - np.arange(2 * P)[None]
    seen = (diff >= 0) & (diff < P)
    con[:, K_M1:K_M1 + 2 * P] = np.where(seen, 0.0, -1e30)
    con[:, K_M0:K_M0 + 2 * P] = np.where(seen & (np.arange(2 * P)[None] >= P), 0.0, -1e30)
    inv = np.float32(10000.0) ** (-np.arange(0, HEAD, 2, dtype=np.float32) / np.float32(HEAD))
    con[:, K_INV] = inv[k % half]
    return con


def build_trunk(nc, stream, ada, params_d, keys_d, con_d, x_d, c_d, pos_d, c_scr, g_scr, out_d):
    with ExitStack() as ctx:
        region_base = [nc.sbuf_base]

        def at(name, off_kb, shape, dt=F32):
            return nc.alloc_sbuf_tensor_at(name, shape, dt, offset=off_kb)

        def sem(name):
            return ctx.enter_context(nc.semaphore(name))

        cur = [-(-region_base[0] // 64) * 64]

        def keep(name, shape, dt=F32):
            n = 4
            for d in shape[1:]:
                n *= d
            t = at(name, cur[0], shape, dt)
            cur[0] += -(-n // 64) * 64
            return t

        xT = keep("xT", [P, C, T])
        h_hi = keep("h_hi", [P, C, T], F32R)
        h_lo = keep("h_lo", [P, C, T], F32R)
        raw = keep("raw", [P, 4, C, P])
        w_hi = keep("w_hi", [P, 2, C, P], F32R)
        w_lo = keep("w_lo", [P, 2, C, P], F32R)
        con = keep("con", [P, NCON])
        params = keep("params", [P, DEPTH, PL])
        lp = keep("lp", [P, PL])
        mod = keep("mod", [P, DEPTH, 6 * C])
        md = keep("md", [P, 6 * C])
        gs = keep("gs", [P, 2, C])
        macc = keep("macc", [P, 4])
        spare = keep("spare", [P, 16])
        st4 = keep("st4", [P, 6, R])
        cosT = keep("cosT", [P, T])
        sinT = keep("sinT", [P, T])
        rstd = keep("rstd", [P, T])
        sq = keep("sq", [P, 2, T])
        hx = keep("hx", [P, 2, T])
        hs = keep("hs", [P, 2, T])
        sg = keep("sg", [P, 2, T])
        cur[0] = -(-cur[0] // 64) * 64
        base = cur[0]
        KB = 1024
        assert base + 91 * KB <= nc.sbuf_usable_end, (base, nc.sbuf_usable_end)
        o_hi = at("o_hi", base, [P, C, T], F32R)
        o_lo = at("o_lo", base + 16 * KB, [P, C, T], F32R)
        qT = at("qT", base + 32 * KB, [P, C, T])
        kT = at("kT", base + 48 * KB, [P, 2, P + T])
        vn = at("vn", base + 53 * KB, [P, NB + 1, NKV * HEAD])
        uT = at("uT", base + 58 * KB, [P, C, PAD + T])
        n_hi = at("n_hi", base + 58 * KB, [P, C, T], F32R)
        yT = at("yT", base + 75 * KB, [P, C, T])
        n_lo = at("n_lo", base + 75 * KB, [P, C, T], F32R)
        vT = at("vT", base + 75 * KB, [P, 2, T])
        scores_sb = [at("sc", base + 83 * KB, [P, R, 2 * P]), hs[:].rearrange("p a (b k) -> p (a b) k", b=2)]
        pT = at("pT", base + 87 * KB, [P, 2, R, P])
        cact = at("cact", base, [P, D])
        junk = at("junk", base + 4 * KB, [P, D])
        pos_i = at("pos_i", base + 8 * KB, [P, T], I32)
        ang = at("ang", base + 10 * KB, [P, T])
        turn = at("turn", base + 12 * KB, [P, T])
        S_all = at("S_all", base, [P, NB, 2 * RH, NKEYS])
        qk = at("qk", base + 32 * KB, [P, 2 * RH, T])
        s_w = at("s_w", base + 32 * KB, [P, 2 * RH, NKEYS])
        eq = at("eq", base + 32 * KB, [P, RH * TOPK, TOPK])
        cand = at("cand", base + 40 * KB, [P, RH, TOPK * TOPK])
        small = base + 48 * KB
        v16 = at("v16", small, [P, 2 * RH, TOPK])
        i16 = at("i16", small + 1024, [P, 2 * RH, TOPK], U32)
        i16f = at("i16f", small + 2048, [P, 2 * RH, TOPK])
        t16 = at("t16", small + 3072, [P, RH, TOPK])
        p16 = at("p16", small + 3584, [P, RH, TOPK], U32)
        ab = at("ab", small + 4096, [P, 2, RH * TOPK], U32)
        abf = at("abf", small + 5120, [P, 2, RH * TOPK])
        routed = at("routed", small + 6144, [P, 3, RH * TOPK])
        esum = at("esum", small + 7680, [P, 2, RH])
        ijg = at("ijg", base + 64 * KB, [P, 3, T])
        g_out = at("g_out", base + 70 * KB, [P, 2, T])
        stage = at("stage", base, [P, NKEYS, P])
        keys = at("keys", base + 74 * KB, [P, 2 * RH, NKEYS])
        oneL = at("oneL", base + 74 * KB, [P, 16, P])
        oneR = at("oneR", base + 82 * KB, [P, 16, P])
        cg = at("cg", base, [P, 4, 2, T])
        coef = at("coef", base + 16 * KB, [P, 2, T])
        cf_hi = at("cf_hi", base + 20 * KB, [P, 2, T], F32R)
        cf_lo = at("cf_lo", base + 24 * KB, [P, 2, T], F32R)

        ps = ctx.enter_context(nc.psum_tensor("ps", [P, 8, 512], F32))
        ident = con[:, K_ID:K_ID + P]
        ones = con[:, K_ONE:K_ONE + P]
        iota = con[:, K_IOTA:K_IOTA + P]

        loaded = [sem(f"tile_loaded{s}") for s in range(4)]
        hi_done = sem("hi_done")
        lo_done = sem("lo_done")
        tile_done = sem("tile_done")
        bank_read = [sem(f"bank_read{b}") for b in range(2)]
        primed = sem("primed")
        const_in = sem("const_in")
        x_in = sem("x_in")
        ada_in = [sem(f"ada_in{s}") for s in range(4)]
        c_silu = sem("c_silu")
        mod_step = sem("mod_step")
        mod_add = sem("mod_add")
        rope_step = sem("rope_step")
        rope_sin = sem("rope_sin")
        lay = sem("lay")
        x_upd = sem("x_upd")
        sq_done = sem("sq_done")
        sq_used = sem("sq_used")
        ms_done = sem("ms_done")
        rt_done = sem("rt_done")
        rs_done = sem("rs_done")
        hx_done = sem("hx_done")
        hs_done = sem("hs_done")
        hhi_done = sem("hhi_done")
        h_ready = sem("h_ready")
        qsq = sem("qsq")
        qss = sem("qss")
        qms = sem("qms")
        qrt = sem("qrt")
        qrs = sem("qrs")
        qn = sem("qn")
        rot = sem("rot")
        qa = sem("qa")
        qcos = sem("qcos")
        qrope = sem("qrope")
        pad0 = sem("pad0")
        v_tr = sem("v_tr")
        v_ev = sem("v_ev")
        s_mm = sem("s_mm")
        s_msk = sem("s_msk")
        a_max = sem("a_max")
        a_neg = sem("a_neg")
        a_exp = sem("a_exp")
        a_den = sem("a_den")
        a_nrm = sem("a_nrm")
        p_tr = sem("p_tr")
        p_ev = sem("p_ev")
        o_mm = sem("o_mm")
        o_hid = sem("o_hid")
        o_lod = sem("o_lod")
        conv_step = sem("conv_step")
        ln_mm = sem("ln_mm")
        ln_step = sem("ln_step")
        ln_sq = sem("ln_sq")
        ln_silu = sem("ln_silu")
        ln_hi = sem("ln_hi")
        ln_lo = sem("ln_lo")
        mrg = sem("mrg")
        mrg_hi = sem("mrg_hi")
        mrg_lo = sem("mrg_lo")
        key_in = sem("key_in")
        r_mm = sem("r_mm")
        r_ev = sem("r_ev")
        top_step = sem("top_step")
        g_exp = sem("g_exp")
        rt_ready = sem("rt_ready")
        rt_tr = sem("rt_tr")
        rt_ev = sem("rt_ev")
        g_st = [sem(f"gelu_stored{s}") for s in range(2)]
        lr_done = sem("lr_done")
        c_mm = sem("c_mm")
        c_ev = sem("c_ev")
        c_st = sem("c_stored")
        cg_in = [sem(f"cg_in{s}") for s in range(4)]
        cg_free = sem("cg_free")
        cf_hid = sem("cf_hid")
        cf_ready = sem("cf_ready")
        out_st = sem("out_st")

        block = ctx.enter_context(nc.Block())

        @block.sync
        def _(sp):
            sp.dma_start(con[:], con_d).then_inc(const_in, 16)
            sp.dma_start(params[:], params_d).then_inc(const_in, 16)
            sp.dma_start(cact[:], c_d.broadcast_to([P, D])).then_inc(const_in, 16)
            sp.dma_start(pos_i[:], pos_d.broadcast_to([P, T])).then_inc(const_in, 16)
            sp.dma_start(xT[:], x_d).then_inc(x_in, 16)
            for s in range(4):
                sp.dma_start(raw[:, s], ada[s]).then_inc(ada_in[s], 16)
            with sp.Fori(1, DEPTH * 6 * C // 4) as r:
                for s in range(4):
                    n = sp.snap(4 * r + s)
                    sp.wait_ge(mod_step, 4 * r + s - 2)
                    sp.dma_start(raw[:, s], ada[n]).then_inc(ada_in[s], 16)
            sp.wait_ge(mod_step, DEPTH * 6 * C + 1)
            sp.wait_ge(primed, 1)

            with sp.Fori(0, DEPTH) as l:
                def load(s, g):
                    n = sp.snap(g)
                    sp.wait_ge(lo_done, n + 1)
                    sp.dma_start(raw[:, s], stream[n]).then_inc(loaded[s], 16)

                with sp.Fori(0, I_W // 4) as r:
                    for s in range(4):
                        load(s, l * NT + 4 * r + s)
                for s in range(4):
                    load(s, l * NT + I_W + s)
                def load_cg(s, j, k):
                    jj = sp.snap(j)
                    sp.wait_ge(cg_free, k)
                    sp.dma_start(cg[:, s, 0], c_scr[jj]).then_inc(cg_in[s], 16)
                    sp.dma_start(cg[:, s, 1], g_scr[jj]).then_inc(cg_in[s], 16)

                with sp.Fori(0, NKEYS // 4 - 1) as r:
                    for s in range(4):
                        load_cg(s, 4 * r + s, l * (NKEYS + 4) + 4 * r + s + 1)
                        load(s, l * NT + I_W + 4 * r + s + 4)
                for s in range(4):
                    load_cg(s, NKEYS - 4 + s, l * (NKEYS + 4) + NKEYS - 4 + s + 1)

            sp.wait_ge(x_upd, DEPTH * C)
            sp.dma_start(out_d, xT[:]).then_inc(out_st, 16)
            sp.wait_ge(out_st, 16)

        @block.gpsimd
        def _(pool):
            nc.gpsimd.memset(spare[:, 15:16], 0.0).then_inc(lo_done, 4)
            with pool.Fori(0, DEPTH) as l:
                def low(s, g):
                    through, high = pool.snap(g + 3), pool.snap(g + 1)
                    pool.wait_ge(tile_done, through)
                    pool.wait_ge(hi_done, high)
                    nc.gpsimd.tensor_tensor(w_lo[:, s % 2], raw[:, s], w_hi[:, s % 2].bitcast(F32),
                                            ALU.subtract).then_inc(lo_done, 1)

                def h_low(w):
                    for c in range(C):
                        n = (2 * l + w) * C + c + 1
                        pool.wait_ge(hhi_done, n)
                        nc.gpsimd.tensor_tensor(h_lo[:, c], hs[:, c % 2], h_hi[:, c].bitcast(F32),
                                                ALU.subtract).then_inc(h_ready, 1)

                for i in range(2):
                    low(i, l * NT + i)
                h_low(0)
                nc.gpsimd.memset(kT[:, :, 0:P], 0.0).then_inc(pad0, 1)
                nc.gpsimd.memset(vn[:, 0], 0.0).then_inc(pad0, 1)
                nc.gpsimd.memset(uT[:, :, 0:PAD], 0.0).then_inc(pad0, 1)
                for i in range(2, 4):
                    low(i, l * NT + i)
                with pool.Fori(1, I_CG // 4) as r:
                    for s in range(4):
                        low(s, l * NT + 4 * r + s)
                for i in range(I_CG, I_CG + 2):
                    low(i % 4, l * NT + i)
                for c in range(C):
                    pool.wait_ge(ln_hi, l * C + c + 1)
                    nc.gpsimd.tensor_tensor(n_lo[:, c], hs[:, c % 2], n_hi[:, c].bitcast(F32),
                                            ALU.subtract).then_inc(ln_lo, 1)
                for m in range(C):
                    for i in range(I_CG + 2 + 2 * m, I_CG + 4 + 2 * m):
                        low(i % 4, l * NT + i)
                    pool.wait_ge(mrg_hi, l * C + m + 1)
                    nc.gpsimd.tensor_tensor(o_lo[:, m], hx[:, m % 2], o_hi[:, m].bitcast(F32),
                                            ALU.subtract).then_inc(mrg_lo, 1)
                for i in range(I_OUT + 2, I_QRY + 2):
                    low(i % 4, l * NT + i)
                h_low(1)
                for i in range(I_QRY + 2, I_QRY + 4):
                    low(i % 4, l * NT + i)
                with pool.Fori(I_QRY // 4 + 1, NT // 4) as r:
                    for s in range(4):
                        low(s, l * NT + 4 * r + s)

        @block.tensor
        def _(pe):
            pe.wait_ge(const_in, 64)
            with pe.Fori(0, DEPTH) as l:
                def read_no(i):
                    return l * (NE // 2) + i // 2 + 2

                def product(s, g, e, hi, lo, ready=None):
                    b = s % 2
                    if ready is not None:
                        pe.wait_ge(*ready)
                    pe.wait_ge(bank_read[b], e)
                    pe.wait_ge(lo_done, g + 5)
                    for c in range(C):
                        wh, wl = w_hi[:, b, c], w_lo[:, b, c]
                        nc.tensor.matmul(ps[:, b], wh, hi[:, c], start=c == 0, stop=False)
                        nc.tensor.matmul(ps[:, b], wh, lo[:, c], start=False, stop=False)
                        mm = nc.tensor.matmul(ps[:, b], wl, hi[:, c], start=False, stop=c == C - 1)
                    mm.then_inc(tile_done, 1)

                def proj(i, hi, lo):
                    product(i % 4, l * NT + i, l * (NE // 2) + i // 2 + 1, hi, lo)

                def proj_loop(i0, i1, hi, lo, ready=None):
                    with pe.Fori(i0 // 4, i1 // 4) as r:
                        for s in range(4):
                            product(s, l * NT + 4 * r + s, l * (NE // 2) + 2 * r + s // 2 + 1, hi, lo,
                                    ready if s == 0 else None)

                def norm_sums(w):
                    for c in range(C):
                        pe.wait_ge(sq_done, (2 * l + w) * C + c + 1)
                        nc.tensor.matmul(ps[:, 7], ones, sq[:, c % 2], start=c == 0,
                                         stop=c == C - 1).then_inc(sq_used, 1)

                norm_sums(0)
                pe.wait_ge(h_ready, 2 * l * C + C)

                def rms_sum(k):
                    pe.wait_ge(qsq, l * 10 + k + 1)
                    if k >= 1:
                        pe.wait_ge(qms, l * 10 + k)
                    nc.tensor.matmul(ps[:, 7], con[:, K_BLK:K_BLK + P], sq[:, k % 2],
                                     start=True, stop=True).then_inc(qss, 1)

                def rotate(k):
                    pe.wait_ge(qn, l * 10 + k + 1)
                    if k >= 1:
                        pe.wait_ge(qa, l * 10 + k)
                    nc.tensor.matmul(ps[:, 6], con[:, K_PERM:K_PERM + P], hx[:, k % 2],
                                     start=True, stop=True).then_inc(rot, 1)

                for i in range(I_GLU + 2):
                    proj(i, h_hi, h_lo)
                    if 1 <= i <= 10:
                        rms_sum(i - 1)
                    if 2 <= i <= 11:
                        rotate(i - 2)
                pe.wait_ge(bank_read[1], read_no(I_GLU - 1))
                for n in range(NB):
                    if n >= 1:
                        pe.wait_ge(v_ev, l * NB + n)
                    for p in range(2):
                        mm = nc.tensor.transpose(ps[:, 2, p * P:(p + 1) * P], vT[:, p, n * P:(n + 1) * P], ident)
                    mm.then_inc(v_tr, 1)

                units = [(n, g) for n in range(NB) for g in range(NKV)]

                def scores(u):
                    n, g = units[u]
                    p, lo64 = g // 2, (g % 2) * HEAD
                    if u >= 1:
                        pe.wait_ge(s_msk, l * 16 + u)
                    for r in range(R):
                        mm = nc.tensor.matmul(ps[:, 2 + r // 2, (r % 2) * 256:(r % 2) * 256 + 256],
                                              qT[lo64:lo64 + HEAD, p * R + r, n * P:(n + 1) * P],
                                              kT[lo64:lo64 + HEAD, p, n * P:(n + 2) * P],
                                              start=True, stop=True)
                    mm.then_inc(s_mm, 1)

                def values(u):
                    n, g = units[u]
                    lo64 = (g % 2) * HEAD
                    pe.wait_ge(a_nrm, l * 16 + u + 1)
                    if u >= 1:
                        pe.wait_ge(p_ev, l * 32 + 2 * u)
                    for kb in range(2):
                        for r in range(R):
                            mm = nc.tensor.transpose(ps[:, 4 + kb, r * P:(r + 1) * P],
                                                     scores_sb[u % 2][:, r, kb * P:(kb + 1) * P], ident)
                        mm.then_inc(p_tr, 1)
                    if u >= 1:
                        pe.wait_ge(o_lod, l * 16 + u)
                    for kb in range(2):
                        pe.wait_ge(p_ev, l * 32 + 2 * u + kb + 1)
                        mm = nc.tensor.matmul(ps[lo64:lo64 + HEAD, 6], vn[:, n + kb, g * HEAD:(g + 1) * HEAD],
                                              pT[:, kb].rearrange("k r q -> k (r q)"),
                                              start=kb == 0, stop=kb == 1)
                    mm.then_inc(o_mm, 1)

                pe.wait_ge(qrope, l * 10 + 10)
                pe.wait_ge(v_ev, l * NB + NB)
                pe.wait_ge(pad0, 3 * l + 3)
                scores(0)
                for u in range(len(units)):
                    if u + 1 < len(units):
                        scores(u + 1)
                    if u < GLU_LATE:
                        proj(I_GLU + 2 + u, h_hi, h_lo)
                    values(u)
                def pairs(i0, hi, lo, ready):
                    with pe.Fori(i0 // 4, i0 // 4 + 4) as r:
                        for s in range(4):
                            a, b = (hi, lo) if s % 2 == 0 else (h_hi, h_lo)
                            product(s, l * NT + 4 * r + s, l * (NE // 2) + 2 * r + s // 2 + 1, a, b,
                                    ready if s == 0 else None)

                pairs(I_AG, o_hi, o_lo, (o_lod, l * 16 + 16))
                for k in range(2):
                    for c in range(C):
                        if k == 0:
                            pe.wait_ge(conv_step, l * C * TAPS + (c // 2 + 1) * 2 * TAPS)
                            nc.tensor.matmul(ps[:, 7], ones, yT[:, c], start=c == 0, stop=c == C - 1).then_inc(ln_mm, 1)
                        else:
                            pe.wait_ge(ln_sq, l * C + c + 1)
                            nc.tensor.matmul(ps[:, 6], ones, sq[:, c % 2], start=c == 0, stop=c == C - 1).then_inc(ln_mm, 1)
                pairs(I_CG, n_hi, n_lo, (ln_lo, l * C + C))
                proj_loop(I_OUT, I_QRY, o_hi, o_lo, (mrg_lo, l * C + C))
                norm_sums(1)
                proj_loop(I_QRY, I_U, h_hi, h_lo, (h_ready, 2 * l * C + 2 * C))
                pe.wait_ge(key_in, 16 * l + 16)
                for b in range(2):
                    pe.wait_ge(bank_read[b], read_no(I_U - 2 + b))
                for tt in range(NB):
                    for q in range(4):
                        if tt >= 1:
                            pe.wait_ge(r_ev, l * 16 + (tt - 1) * 4 + q + 1)
                        for k in range(4):
                            hp = 4 * q + k
                            mm = nc.tensor.matmul(ps[:, 2 + q, k * P:(k + 1) * P], qk[:, hp, tt * P:(tt + 1) * P],
                                                  keys[:, hp], start=True, stop=True)
                        mm.then_inc(r_mm, 1)
                with pe.Fori(0, NB) as tt:
                    with pe.Fori(0, 4) as r:
                        for s in range(4):
                            product(s, l * NT + I_U + 16 * tt + 4 * r + s,
                                    l * (NE // 2) + I_U // 2 + 8 * tt + 2 * r + s // 2 + 1, h_hi, h_lo)
                    pe.wait_ge(rt_ready, l * NB + tt + 1)
                    for k in range(3):
                        mm = nc.tensor.transpose(ps[:, 6, k * P:(k + 1) * P], routed[:, k], ident)
                    mm.then_inc(rt_tr, 1)
                with pe.Fori(0, NB) as tb:
                    with pe.Fori(0, 2) as r:
                        for s in range(4):
                            product(s, l * NT + I_U + 64 + 16 * tb + 4 * r + s,
                                    l * (NE // 2) + I_U // 2 + 32 + 8 * tb + 2 * r + s // 2 + 1, h_hi, h_lo)
                            for q in range(4):
                                n4 = l * 128 + 32 * tb + 16 * r + 4 * s + q
                                pe.wait_ge(c_ev, n4 + 1)
                                pe.wait_ge(lr_done, n4 + 1)
                                for k in range(4):
                                    mm = nc.tensor.matmul(ps[:, 2 + q, k * P:(k + 1) * P], oneL[:, 4 * q + k],
                                                          oneR[:, 4 * q + k], start=True, stop=True)
                                mm.then_inc(c_mm, 1)
                    with pe.Fori(0, 2) as r:
                        for s in range(4):
                            product(s, l * NT + I_U + 72 + 16 * tb + 4 * r + s,
                                    l * (NE // 2) + I_U // 2 + 36 + 8 * tb + 2 * r + s // 2 + 1, h_hi, h_lo)

                def experts(s, j, g, first, last):
                    b = s % 2
                    pe.wait_ge(cf_ready, j + 5)
                    pe.wait_ge(lo_done, g + 5)
                    for c in range(C):
                        nc.tensor.matmul(ps[:, c], w_hi[:, b, c], cf_hi[:, b], start=first, stop=False)
                        nc.tensor.matmul(ps[:, c], w_hi[:, b, c], cf_lo[:, b], start=False, stop=False)
                        mm = nc.tensor.matmul(ps[:, c], w_lo[:, b, c], cf_hi[:, b], start=False, stop=last)
                    mm.then_inc(tile_done, 1)

                for b in range(2):
                    pe.wait_ge(bank_read[b], (l + 1) * (NE // 2) + 1)
                pe.wait_ge(c_ev, (l + 1) * 128 + 4)
                pe.wait_ge(rt_ev, (l + 1) * NB)
                for s in range(4):
                    experts(s, l * NKEYS + s, l * NT + I_W + s, s == 0, False)
                with pe.Fori(1, NKEYS // 4 - 1) as r:
                    for s in range(4):
                        experts(s, l * NKEYS + 4 * r + s, l * NT + I_W + 4 * r + s, False, False)
                for s in range(4):
                    j = NKEYS - 4 + s
                    experts(s, l * NKEYS + j, l * NT + I_W + j, False, s == 3)

        @block.scalar
        def _(act):
            act.wait_ge(const_in, 64)
            nc.scalar.activation(cact[:], cact[:], ACT.Silu).then_inc(c_silu, 1)
            for k, dst in enumerate((sinT, cosT)):
                act.wait_ge(rope_sin, 2 * k + 1)
                nc.scalar.activation(dst[:], turn[:], ACT.Sin).then_inc(rope_sin, 1)
            act.wait_ge(primed, 1)
            act.wait_ge(x_in, 16)
            with act.Fori(0, DEPTH) as l:
                def read_no(i):
                    return l * (NE // 2) + i // 2 + 2

                def high(s, g):
                    act.wait_ge(tile_done, g + 3)
                    nc.scalar.copy(w_hi[:, s % 2], raw[:, s]).then_inc(hi_done, 1)

                def high_at(i):
                    act.wait_ge(loaded[i % 4], (l * (NT // 4) + i // 4 + 1) * 16)
                    high(i % 4, l * NT + i)

                def high_in(s, i0, r):
                    act.wait_ge(loaded[s], (l * (NT // 4) + r + i0 // 4 + 1) * 16)
                    high(s, l * NT + i0 + 4 * r)

                def norm(w):
                    for c in range(C):
                        n = (2 * l + w) * C + c
                        if w == 1:
                            act.wait_ge(bank_read[c % 2], read_no(I_OUT + c))
                        if c >= 2:
                            act.wait_ge(sq_used, (2 * l + w) * C + c - 1)
                        nc.scalar.activation(sq[:, c % 2], xT[:, c], ACT.Square).then_inc(sq_done, 1)
                    act.wait_ge(ms_done, 2 * l + w + 1)
                    nc.scalar.activation(rstd[:], rstd[:], ACT.Sqrt).then_inc(rt_done, 1)
                    for c in range(C):
                        n = (2 * l + w) * C + c
                        act.wait_ge(hx_done, n + 1)
                        if c >= 2:
                            act.wait_ge(h_ready, (2 * l + w) * C + c - 1)
                        nc.scalar.activation(hs[:, c % 2], hx[:, c % 2], ACT.Identity, scale=gs[:, w, c:c + 1],
                                             bias=md[:, 3 * w * C + c:3 * w * C + c + 1]).then_inc(hs_done, 1)
                        act.wait_ge(hs_done, n + 1)
                        nc.scalar.copy(h_hi[:, c], hs[:, c % 2]).then_inc(hhi_done, 1)

                high_at(0)
                high_at(1)
                act.wait_ge(lay, 2 * l + 2)
                norm(0)

                def q_root(k):
                    act.wait_ge(qms, l * 10 + k + 1)
                    nc.scalar.activation(hs[:, k % 2], hs[:, k % 2], ACT.Sqrt).then_inc(qrt, 1)

                for i in range(I_GLU):
                    high_at(i + 2)
                    act.wait_ge(tile_done, l * NT + i + 5)
                    dst = qT[:, i] if i < I_K else kT[:, i - I_K, P:P + T] if i < I_V else vT[:, i - I_V]
                    nc.scalar.copy(dst, ps[:, i % 2]).then_inc(bank_read[i % 2], 1)
                    if i < I_V:
                        if i >= 2:
                            act.wait_ge(qss, l * 10 + i - 1)
                        act.wait_ge(bank_read[i % 2], read_no(i))
                        nc.scalar.activation(sq[:, i % 2], dst, ACT.Square).then_inc(qsq, 1)
                    if 1 <= i <= 10:
                        q_root(i - 1)

                def sigmoid(s, i):
                    act.wait_ge(bank_read[0], read_no(i - 5))
                    act.wait_ge(tile_done, l * NT + i + 5)
                    nc.scalar.activation(sg[:, (s // 2) % 2], ps[:, 1], ACT.Sigmoid).then_inc(bank_read[1], 1)

                def sigmoid_in(s, i0, r):
                    act.wait_ge(bank_read[0], l * (NE // 2) + (i0 + s - 5) // 2 + 2 * r + 2)
                    act.wait_ge(tile_done, l * NT + i0 + s + 4 * r + 5)
                    nc.scalar.activation(sg[:, s // 2], ps[:, 1], ACT.Sigmoid).then_inc(bank_read[1], 1)

                act.wait_ge(qrope, l * 10 + 10)
                def glu_tile(i):
                    high_at(i + 2)
                    if i % 2 == 1:
                        sigmoid(i - I_GLU, i)

                def probs(u):
                    sc = scores_sb[u % 2]
                    act.wait_ge(a_den, 3 * (l * 16 + u) + 1)
                    act.wait_ge(a_neg, l * 16 + u + 1)
                    for r in range(R):
                        nc.scalar.activation(sc[:, r], sc[:, r], ACT.Exp, bias=st4[:, 1, r:r + 1],
                                             accum_out=st4[:, 2, r:r + 1])
                    nc.scalar.activation(st4[:, 4], st4[:, 3], ACT.Exp).then_inc(a_exp, 1)

                glu_tile(I_GLU)
                glu_tile(I_GLU + 1)
                probs(0)
                for u in range(16):
                    n, g = u // NKV, u % NKV
                    p, lo64 = g // 2, (g % 2) * HEAD
                    if u < 15:
                        probs(u + 1)
                    if u < GLU_LATE:
                        glu_tile(I_GLU + 2 + u)
                    act.wait_ge(p_tr, l * 32 + 2 * u + 1)
                    if u >= 1:
                        act.wait_ge(o_mm, l * 16 + u)
                    nc.scalar.copy(pT[:, 0], ps[:, 4].rearrange("k (r q) -> k r q", r=R)).then_inc(p_ev, 1)
                    act.wait_ge(p_tr, l * 32 + 2 * u + 2)
                    nc.scalar.copy(pT[:, 1], ps[:, 5].rearrange("k (r q) -> k r q", r=R)).then_inc(p_ev, 1)
                    act.wait_ge(o_mm, l * 16 + u + 1)
                    nc.scalar.copy(o_hi[lo64:lo64 + HEAD, p * R:(p + 1) * R, n * P:(n + 1) * P],
                                   ps[lo64:lo64 + HEAD, 6].rearrange("f (r q) -> f r q", r=R)).then_inc(o_hid, 1)
                with act.Fori(0, 4) as r:
                    for s in range(4):
                        high_in((s + 2) % 4, I_AG + s + 2, r)
                        if s % 2 == 1:
                            sigmoid_in(s, I_AG, r)
                for c in range(C):
                    act.wait_ge(ln_step, l * LN_STEPS + 1 + c + 1)
                    if c >= 2:
                        act.wait_ge(ln_mm, l * 2 * C + C + c - 1)
                    nc.scalar.activation(sq[:, c % 2], yT[:, c], ACT.Square).then_inc(ln_sq, 1)
                act.wait_ge(ln_step, l * LN_STEPS + C + 2)
                nc.scalar.activation(rstd[:], rstd[:], ACT.Sqrt).then_inc(ln_silu, 1)
                for c in range(C):
                    act.wait_ge(ln_step, l * LN_STEPS + C + 3 + c + 1)
                    if c >= 2:
                        act.wait_ge(ln_lo, l * C + c - 1)
                    nc.scalar.activation(hs[:, c % 2], hx[:, c % 2], ACT.Silu, scale=lp[:, O_LG + c:O_LG + c + 1],
                                         bias=lp[:, O_LB + c:O_LB + c + 1]).then_inc(ln_silu, 1)
                    act.wait_ge(ln_silu, l * (C + 1) + 1 + c + 1)
                    nc.scalar.copy(n_hi[:, c], hs[:, c % 2]).then_inc(ln_hi, 1)
                for m in range(C):
                    i = I_CG + 2 * m
                    high_at(i + 2)
                    high_at(i + 3)
                    sigmoid(2 * (m % 2) + 1, i + 1)
                    act.wait_ge(mrg, l * C + m + 1)
                    nc.scalar.copy(o_hi[:, m], hx[:, m % 2]).then_inc(mrg_hi, 1)
                for i in range(I_OUT, I_QRY):
                    high_at(i + 2)
                norm(1)
                ll = act.snap(l + 0)
                act.wait_ge(bank_read[1], read_no(I_QRY - 1))
                act.dma_start(keys[:], keys_d[ll]).then_inc(key_in, 16)
                for i in range(I_QRY, I_U):
                    high_at(i + 2)
                    act.wait_ge(tile_done, l * NT + i + 5)
                    nc.scalar.copy(qk[:, i - I_QRY], ps[:, i % 2]).then_inc(bank_read[i % 2], 1)
                for n in range(16):
                    act.wait_ge(r_mm, l * 16 + n + 1)
                    nc.scalar.copy(S_all[:, n // 4, 4 * (n % 4):4 * (n % 4) + 4],
                                   ps[:, 2 + n % 4].rearrange("t (k n) -> t k n", k=4)).then_inc(r_ev, 1)

                def gelu(s, j, nth, g):
                    jj = act.snap(j)
                    act.wait_ge(g_st[s % 2], (l * (NKEYS // 2) + nth) * 16 + 16)
                    act.wait_ge(tile_done, g + 5)
                    nc.scalar.activation(g_out[:, s % 2], ps[:, s % 2], ACT.Gelu).then_inc(bank_read[s % 2], 1)
                    act.wait_ge(bank_read[s % 2], l * (NE // 2) + I_U // 2 + nth + 2)
                    act.dma_start(g_scr[jj], g_out[:, s % 2]).then_inc(g_st[s % 2], 16)

                with act.Fori(0, NB) as tt:
                    with act.Fori(0, 4) as r:
                        for s in range(4):
                            high_in((s + 2) % 4, I_U + s + 2, 4 * tt + r)
                            gelu(s, 16 * tt + 4 * r + s, 8 * tt + 2 * r + s // 2,
                                 l * NT + I_U + 16 * tt + 4 * r + s)
                    act.wait_ge(g_exp, 2 * (l * NB + tt) + 1)
                    nc.scalar.activation(t16[:], t16[:], ACT.Exp).then_inc(g_exp, 1)
                with act.Fori(0, NB) as tb:
                    with act.Fori(0, 2) as r:
                        for s in range(4):
                            high_in((s + 2) % 4, I_U + 64 + s + 2, 4 * tb + r)
                            gelu(s, 64 + 16 * tb + 4 * r + s, 32 + 8 * tb + 2 * r + s // 2,
                                 l * NT + I_U + 64 + 16 * tb + 4 * r + s)
                            if s == 0:
                                act.wait_ge(c_st, (l * NB + tb) * 64 + 64)
                            for q in range(4):
                                t0 = act.snap(64 * r + 16 * s + 4 * q)
                                act.wait_ge(c_mm, l * 128 + 32 * tb + 16 * r + 4 * s + q + 5)
                                nc.scalar.copy(stage[:, :, bass.ds(t0, 4)].rearrange("i j t -> i t j"),
                                               ps[:, 2 + q].rearrange("i (t j) -> i t j", t=4)).then_inc(c_ev, 1)
                    tb0 = act.snap(P * tb)
                    act.wait_ge(c_ev, l * 128 + 32 * tb + 32 + 4)
                    for k in range(4):
                        act.dma_start(c_scr[32 * k:32 * k + 32, :, bass.ds(tb0, P)].rearrange("j i t -> i j t"),
                                      stage[:, 32 * k:32 * k + 32]).then_inc(c_st, 16)
                    with act.Fori(0, 2) as r:
                        for s in range(4):
                            high_in((s + 2) % 4, I_U + 72 + s + 2, 4 * tb + r)
                            gelu(s, 72 + 16 * tb + 4 * r + s, 36 + 8 * tb + 2 * r + s // 2,
                                 l * NT + I_U + 72 + 16 * tb + 4 * r + s)
                for b in range(2):
                    act.wait_ge(g_st[b], (l + 1) * (NKEYS // 2 * 16) + 16)
                act.wait_ge(c_st, (l + 1) * (NB * 64) + 64)
                nc.scalar.copy(st4[:, 4], st4[:, 3]).then_inc(cg_free, 4)
                for i in range(I_W + 2, I_W + 4):
                    high_at(i)
                with act.Fori(0, NKEYS // 4 - 1) as r:
                    for s in range(4):
                        high_in(s, I_W + 4 + s, r)

        @block.vector
        def _(dve):
            starts = [(bank_read[0], 1), (bank_read[1], 1), (g_st[0], 16), (g_st[1], 16), (tile_done, 4),
                      (c_mm, 4), (c_ev, 4), (cf_ready, 4), (c_st, 64), (mod_step, 1), (mod_add, 1), (primed, 1)]
            for n, (counter, start) in enumerate(starts):
                nc.vector.memset(spare[:, n:n + 1], 0.0).then_inc(counter, start)
            dve.wait_ge(const_in, 64)
            steps = [0]

            def step(ins):
                steps[0] += 1
                ins.then_inc(rope_step, 1)
                dve.wait_ge(rope_step, steps[0])

            step(nc.vector.tensor_copy(ang[:], pos_i[:]))
            step(nc.vector.tensor_scalar(ang[:], ang[:], con[:, K_INV:K_INV + 1], None, ALU.mult))
            for k in range(2):
                if k == 1:
                    dve.wait_ge(rope_sin, 2)
                step(nc.vector.tensor_scalar(turn[:], ang[:], 1 / (2 * np.pi), 0.25 * k, ALU.mult, ALU.add))
                step(nc.vector.tensor_scalar(turn[:], turn[:], MAGIC, None, ALU.add))
                step(nc.vector.tensor_scalar(junk[:, 0:T], turn[:], MAGIC, None, ALU.subtract))
                step(nc.vector.scalar_tensor_tensor(out=turn[:], in0=junk[:, 0:T], scalar=-TP1, in1=ang[:],
                                                    op0=ALU.mult, op1=ALU.add))
                step(nc.vector.scalar_tensor_tensor(out=turn[:], in0=junk[:, 0:T], scalar=-TP2, in1=turn[:],
                                                    op0=ALU.mult, op1=ALU.add))
                step(nc.vector.scalar_tensor_tensor(out=turn[:], in0=junk[:, 0:T], scalar=-TP3, in1=turn[:],
                                                    op0=ALU.mult, op1=ALU.add))
                step(nc.vector.tensor_scalar(turn[:], turn[:], 0.5 * np.pi * k, None, ALU.add))
                nc.vector.tensor_scalar(turn[:], turn[:], PI, -PI, ALU.min, ALU.max).then_inc(rope_sin, 1)
            dve.wait_ge(c_silu, 1)
            with dve.Fori(0, DEPTH * 6 * C // 4) as r:
                for s in range(4):
                    dve.wait_ge(ada_in[s], 16 * r + 16)
                    if s == 0:
                        dve.wait_ge(mod_add, r + 1)
                    dve.wait_ge(mod_step, 4 * r + s + 1)
                    nc.vector.tensor_tensor_reduce(
                        out=junk[:], in0=raw[:, s].rearrange("p c m -> p (c m)"), in1=cact[:], scale=1.0, scalar=0.0,
                        op0=ALU.mult, op1=ALU.add, accum_out=macc[:, s:s + 1]).then_inc(mod_step, 1)
                col = dve.snap(4 * r)
                dve.wait_ge(mod_step, 4 * r + 5)
                nc.vector.tensor_copy(mod[:].rearrange("p l m -> p (l m)")[:, bass.ds(col, 4)],
                                      macc[:]).then_inc(mod_add, 1)
            dve.wait_ge(mod_add, DEPTH * 6 * C // 4 + 1)

            with dve.Fori(0, DEPTH) as l:
                ll = dve.snap(l + 0)
                nc.vector.tensor_copy(lp[:], params[:, bass.ds(ll, 1)].rearrange("p o n -> p (o n)")).then_inc(lay, 1)
                dve.wait_ge(lay, 2 * l + 1)
                nc.vector.tensor_tensor(md[:], mod[:, bass.ds(ll, 1)].rearrange("p o n -> p (o n)"),
                                        lp[:, O_AB:O_AB + 6 * C], ALU.add).then_inc(mod_add, 1)
                dve.wait_ge(mod_add, DEPTH * 6 * C // 4 + 2 * l + 2)
                nc.vector.scalar_tensor_tensor(out=gs[:, 0], in0=md[:, C:2 * C], scalar=1.0, in1=lp[:, 0:C],
                                               op0=ALU.add, op1=ALU.mult).then_inc(mod_add, 1)
                nc.vector.scalar_tensor_tensor(out=gs[:, 1], in0=md[:, 4 * C:5 * C], scalar=1.0, in1=lp[:, C:2 * C],
                                               op0=ALU.add, op1=ALU.mult).then_inc(lay, 1)

                def norm(w):
                    n = 2 * l + w
                    dve.wait_ge(sq_used, n * C + C)
                    nc.vector.tensor_scalar(rstd[:], ps[:, 7], 1.0 / D, EPS, ALU.mult, ALU.add).then_inc(ms_done, 1)
                    dve.wait_ge(rt_done, n + 1)
                    nc.vector.reciprocal(rstd[:], rstd[:]).then_inc(rs_done, 1)
                    dve.wait_ge(rs_done, n + 1)
                    for c in range(C):
                        if c >= 2:
                            dve.wait_ge(hs_done, n * C + c - 1)
                        nc.vector.tensor_tensor(hx[:, c % 2], xT[:, c], rstd[:], ALU.mult).then_inc(hx_done, 1)

                def read_no(i):
                    return l * (NE // 2) + i // 2 + 2

                dve.wait_ge(x_in, 16)
                norm(0)

                def q_dst(k):
                    return qT[:, k] if k < I_K else kT[:, k - I_K, P:P + T]

                def q_ms(k):
                    dve.wait_ge(qss, l * 10 + k + 1)
                    nc.vector.tensor_scalar(hs[:, k % 2], ps[:, 7], 1.0 / HEAD, EPS, ALU.mult, ALU.add).then_inc(qms, 1)

                def q_norm(k):
                    dve.wait_ge(qrt, l * 10 + k + 1)
                    nc.vector.reciprocal(hs[:, k % 2], hs[:, k % 2]).then_inc(qrs, 1)
                    dve.wait_ge(qrs, l * 10 + k + 1)
                    gain = lp[:, O_QG:O_QG + 1] if k < I_K else lp[:, O_KG:O_KG + 1]
                    nc.vector.scalar_tensor_tensor(out=hx[:, k % 2], in0=q_dst(k), scalar=gain, in1=hs[:, k % 2],
                                                   op0=ALU.mult, op1=ALU.mult).then_inc(qn, 1)
                    dve.wait_ge(qn, l * 10 + k + 1)
                    nc.vector.tensor_tensor(q_dst(k), hx[:, k % 2], cosT[:], ALU.mult).then_inc(qcos, 1)

                def q_rot(k):
                    dve.wait_ge(rot, l * 10 + k + 1)
                    if k >= 2:
                        dve.wait_ge(qrope, l * 10 + k - 1)
                    nc.vector.tensor_tensor(sg[:, k % 2], ps[:, 6], sinT[:], ALU.mult).then_inc(qa, 1)
                    dve.wait_ge(qa, l * 10 + k + 1)
                    dve.wait_ge(qcos, l * 10 + k + 1)
                    nc.vector.tensor_tensor(q_dst(k), q_dst(k), sg[:, k % 2], ALU.add).then_inc(qrope, 1)

                dve.wait_ge(h_ready, 2 * l * C + C)
                for k in range(10):
                    q_ms(k)
                    q_norm(k)
                    q_rot(k)
                for n in range(NB):
                    if n == 0:
                        dve.wait_ge(pad0, 3 * l + 3)
                    dve.wait_ge(v_tr, l * NB + n + 1)
                    nc.vector.tensor_copy(vn[:, n + 1], ps[:, 2, 0:2 * P]).then_inc(v_ev, 1)
                def gated(c):
                    dve.wait_ge(bank_read[1], read_no(I_GLU + 2 * c + 1))
                    nc.vector.tensor_tensor(uT[:, c, PAD:PAD + T], ps[:, 0], sg[:, c % 2],
                                            ALU.mult).then_inc(bank_read[0], 1)

                def tap(nth):
                    c, k = 2 * (nth // (2 * TAPS)) + nth % 2, nth // 2 % TAPS
                    weight = lp[:, O_CW + TAPS * c + k:O_CW + TAPS * c + k + 1]
                    if k == 0:
                        dve.wait_ge(bank_read[0], read_no(I_GLU + 2 * c))
                        ins = nc.vector.tensor_scalar(yT[:, c], uT[:, c, 0:T], weight, lp[:, O_CB + c:O_CB + c + 1],
                                                      ALU.mult, ALU.add)
                    else:
                        dve.wait_ge(conv_step, l * C * TAPS + nth - 1)
                        ins = nc.vector.scalar_tensor_tensor(out=yT[:, c], in0=uT[:, c, k:k + T], scalar=weight,
                                                             in1=yT[:, c], op0=ALU.mult, op1=ALU.add)
                    ins.then_inc(conv_step, 1)

                def taps(u, part):
                    n0 = (u - 2) * EARLY_TAPS
                    for nth in range(n0 + part * EARLY_TAPS // 3, n0 + (part + 1) * EARLY_TAPS // 3):
                        if 0 <= nth < EARLY * TAPS:
                            tap(nth)

                def row_stats(u):
                    n, g = u // NKV, u % NKV
                    sc = scores_sb[u % 2]
                    mask = con[:, K_M0:K_M0 + 256] if n == 0 else con[:, K_M1:K_M1 + 256]
                    sink = lp[:, O_SK + g * R:O_SK + (g + 1) * R]
                    k = l * 16 + u + 1
                    dve.wait_ge(s_mm, k)
                    if u >= 2:
                        dve.wait_ge(p_tr, l * 32 + 2 * u - 2)
                    nc.vector.scalar_tensor_tensor(
                        out=sc[:], in0=ps[:, 2:4].rearrange("q b (r k) -> q (b r) k", r=2), scalar=HEAD ** -0.5,
                        in1=mask.rearrange("q (o k) -> q o k", o=1).broadcast_to([P, R, 256]),
                        op0=ALU.mult, op1=ALU.add).then_inc(s_msk, 1)
                    dve.wait_ge(s_msk, k)
                    nc.vector.tensor_reduce(st4[:, 0], sc[:], AX, ALU.max).then_inc(a_max, 1)
                    dve.wait_ge(a_max, 2 * (l * 16 + u) + 1)
                    nc.vector.tensor_tensor(st4[:, 5], st4[:, 0], sink, ALU.max).then_inc(a_max, 1)
                    dve.wait_ge(a_max, 2 * (l * 16 + u) + 2)
                    nc.vector.tensor_tensor(st4[:, 3], sink, st4[:, 5], ALU.subtract).then_inc(a_den, 1)
                    nc.vector.tensor_scalar(st4[:, 1], st4[:, 5], -1.0, None, ALU.mult).then_inc(a_neg, 1)

                def normalise(u):
                    sc = scores_sb[u % 2]
                    dve.wait_ge(a_exp, l * 16 + u + 1)
                    nc.vector.tensor_tensor(st4[:, 0], st4[:, 2], st4[:, 4], ALU.add).then_inc(a_den, 1)
                    dve.wait_ge(a_den, 3 * (l * 16 + u) + 2)
                    nc.vector.reciprocal(st4[:, 5], st4[:, 0]).then_inc(a_den, 1)
                    dve.wait_ge(a_den, 3 * (l * 16 + u) + 3)
                    nc.vector.tensor_tensor(
                        sc[:], sc[:], st4[:, 5].rearrange("q (r o) -> q r o", o=1).broadcast_to([P, R, 256]),
                        ALU.mult).then_inc(a_nrm, 1)

                def attended_low(u):
                    n, g = u // NKV, u % NKV
                    p, lo64 = g // 2, (g % 2) * HEAD
                    dve.wait_ge(o_hid, l * 16 + u + 1)
                    dst = (slice(lo64, lo64 + HEAD), slice(p * R, (p + 1) * R), slice(n * P, (n + 1) * P))
                    nc.vector.tensor_tensor(o_lo[dst], ps[lo64:lo64 + HEAD, 6].rearrange("f (r q) -> f r q", r=R),
                                            o_hi[dst].bitcast(F32), ALU.subtract).then_inc(o_lod, 1)

                gated(0)
                row_stats(0)
                normalise(0)
                for u in range(16):
                    taps(u, 0)
                    if u < 15:
                        row_stats(u + 1)
                    taps(u, 1)
                    if u < 15:
                        normalise(u + 1)
                    if u < GLU_LATE and u % 2 == 1:
                        gated((u + 2) // 2)
                    taps(u, 2)
                    attended_low(u)
                def attn_gated(r, s):
                    c = dve.snap(4 * r + s)
                    dve.wait_ge(bank_read[1], read_no(I_AG + 2 * s + 1) + 4 * r)
                    nc.vector.tensor_tensor(qT[:, bass.ds(c, 1)].rearrange("p o t -> p (o t)"),
                                            ps[:, 0], sg[:, s % 2], ALU.mult).then_inc(bank_read[0], 1)

                with dve.Fori(0, (C - EARLY) // 2) as r:
                    for k in range(TAPS):
                        for s in range(2):
                            c = 2 * r + s + EARLY
                            src = uT[:, bass.ds(c, 1), k:k + T].rearrange("p o t -> p (o t)")
                            dst = yT[:, bass.ds(c, 1)].rearrange("p o t -> p (o t)")
                            tap = lp[:, bass.ds(O_CW + k + TAPS * c, 1)]
                            if k == 0:
                                dve.wait_ge(bank_read[0], read_no(I_AG - 2))
                                ins = nc.vector.tensor_scalar(dst, src, tap, lp[:, bass.ds(O_CB + c, 1)],
                                                              ALU.mult, ALU.add)
                            else:
                                dve.wait_ge(conv_step, (l * C + c - s) * TAPS + 2 * k - 1 + s)
                                ins = nc.vector.scalar_tensor_tensor(out=dst, in0=src, scalar=tap, in1=dst,
                                                                     op0=ALU.mult, op1=ALU.add)
                            ins.then_inc(conv_step, 1)
                        if k in (8, 16, 24, 30):
                            attn_gated(r, -(-k // 8) - 1)
                b0 = l * LN_STEPS
                dve.wait_ge(ln_mm, l * 2 * C + C)
                nc.vector.tensor_scalar(hx[:, 0], ps[:, 7], 1.0 / D, None, ALU.mult).then_inc(ln_step, 1)
                dve.wait_ge(ln_step, b0 + 1)
                for c in range(C):
                    nc.vector.tensor_tensor(yT[:, c], yT[:, c], hx[:, 0], ALU.subtract).then_inc(ln_step, 1)
                dve.wait_ge(ln_mm, l * 2 * C + 2 * C)
                nc.vector.tensor_scalar(rstd[:], ps[:, 6], 1.0 / D, EPS, ALU.mult, ALU.add).then_inc(ln_step, 1)
                dve.wait_ge(ln_silu, l * (C + 1) + 1)
                nc.vector.reciprocal(rstd[:], rstd[:]).then_inc(ln_step, 1)
                dve.wait_ge(ln_step, b0 + C + 3)
                for c in range(C):
                    if c >= 2:
                        dve.wait_ge(ln_silu, l * (C + 1) + 1 + c - 1)
                    nc.vector.tensor_tensor(hx[:, c % 2], yT[:, c], rstd[:], ALU.mult).then_inc(ln_step, 1)
                for m in range(C):
                    dve.wait_ge(bank_read[1], read_no(I_CG + 2 * m + 1))
                    if m >= 2:
                        dve.wait_ge(mrg_lo, l * C + m - 1)
                    else:
                        dve.wait_ge(ln_silu, (l + 1) * (C + 1))
                    nc.vector.tensor_tensor(hx[:, m % 2], ps[:, 0], sg[:, m % 2], ALU.mult).then_inc(bank_read[0], 1)
                    dve.wait_ge(bank_read[0], read_no(I_CG + 2 * m))
                    nc.vector.tensor_tensor(hx[:, m % 2], hx[:, m % 2], qT[:, m], ALU.add).then_inc(mrg, 1)

                with dve.Fori(0, 4) as r:
                    for s in range(2):
                        c = dve.snap(2 * r + s)
                        dve.wait_ge(tile_done, l * NT + I_OUT + 2 * r + s + 5)
                        xc = xT[:, bass.ds(c, 1)].rearrange("p o t -> p (o t)")
                        nc.vector.scalar_tensor_tensor(out=xc, in0=ps[:, s], scalar=md[:, bass.ds(2 * C + c, 1)],
                                                       in1=xc, op0=ALU.mult, op1=ALU.add).then_inc(bank_read[s], 1)
                norm(1)

                with dve.Fori(0, NB) as tt:
                    ttv = dve.snap(tt + 0)
                    tb = l * (NB * TOP_STEPS) + tt * TOP_STEPS
                    count = [0]

                    def mark(ins):
                        count[0] += 1
                        ins.then_inc(top_step, 1)

                    def settle():
                        dve.wait_ge(top_step, tb + count[0])

                    def guard():
                        mark(nc.vector.memset(spare[:, 0:1], 0.0))

                    dve.wait_ge(r_ev, l * 16 + 16)
                    mark(nc.vector.tensor_copy(s_w[:], S_all[:, bass.ds(ttv, 1)].rearrange("t o h n -> t (o h) n")))
                    settle()
                    guard()

                    def top16(vals, ids, src, n):
                        for r8 in range(2):
                            for h in range(n):
                                mark(nc.vector.max(vals[:, h, 8 * r8:8 * r8 + 8], src[:, h]))
                            settle()
                            guard()
                            for h in range(n):
                                mark(nc.vector.max_index(ids[:, h, 8 * r8:8 * r8 + 8], vals[:, h, 8 * r8:8 * r8 + 8],
                                                         src[:, h]))
                            if r8 == 0:
                                settle()
                                guard()
                                for h in range(n):
                                    mark(nc.vector.match_replace(src[:, h], vals[:, h, 0:8], src[:, h], LOWEST))
                                settle()
                                guard()

                    top16(v16, i16, s_w, 2 * RH)
                    v4 = v16[:].rearrange("t (h p) k -> t h p k", p=2)
                    mark(nc.vector.tensor_tensor(
                        cand[:].rearrange("t h (a b) -> t h a b", a=TOPK),
                        v4[:, :, 0].rearrange("t h (k o) -> t h k o", o=1).broadcast_to([P, RH, TOPK, TOPK]),
                        v4[:, :, 1].rearrange("t h (o k) -> t h o k", o=1).broadcast_to([P, RH, TOPK, TOPK]),
                        ALU.add))
                    settle()
                    guard()
                    top16(t16, p16, cand, RH)
                    settle()
                    mark(nc.vector.tensor_copy(esum[:, 0:1].rearrange("t o h -> t h o"), t16[:, :, 0:1]))
                    settle()
                    nc.vector.tensor_tensor(t16[:], t16[:], esum[:, 0].rearrange("t (h o) -> t h o", o=1)
                                            .broadcast_to([P, RH, TOPK]), ALU.subtract).then_inc(g_exp, 1)
                    pos = p16[:].rearrange("t h k -> t (h k)")
                    mark(nc.vector.tensor_scalar(ab[:, 0], pos, 4, None, ALU.logical_shift_right))
                    mark(nc.vector.tensor_scalar(ab[:, 1], pos, TOPK - 1, None, ALU.bitwise_and))
                    mark(nc.vector.tensor_copy(i16f[:], i16[:]))
                    settle()
                    mark(nc.vector.tensor_copy(abf[:], ab[:]))
                    settle()
                    for p in range(2):
                        mark(nc.vector.tensor_tensor(
                            eq[:], abf[:, p].rearrange("t (k o) -> t k o", o=1).broadcast_to([P, RH * TOPK, TOPK]),
                            con[:, K_IOTA:K_IOTA + TOPK].rearrange("t (o a) -> t o a", o=1)
                            .broadcast_to([P, RH * TOPK, TOPK]), ALU.is_equal))
                        settle()
                        i4 = i16f[:].rearrange("t (h p) a -> t h p a", p=2)[:, :, p]
                        e4 = eq[:].rearrange("t (h k) a -> t h k a", h=RH)
                        mark(nc.vector.tensor_tensor(
                            e4, e4, i4.rearrange("t h (o a) -> t h o a", o=1).broadcast_to([P, RH, TOPK, TOPK]),
                            ALU.mult))
                        settle()
                        mark(nc.vector.tensor_reduce(routed[:, p], eq[:], AX, ALU.add))
                        settle()
                    dve.wait_ge(g_exp, 2 * (l * NB + tt) + 2)
                    mark(nc.vector.tensor_reduce(esum[:, 1], t16[:], AX, ALU.add))
                    settle()
                    mark(nc.vector.reciprocal(esum[:, 0], esum[:, 1]))
                    settle()
                    nc.vector.tensor_tensor(routed[:, 2].rearrange("t (h k) -> t h k", h=RH), t16[:],
                                            esum[:, 0].rearrange("t (h o) -> t h o", o=1)
                                            .broadcast_to([P, RH, TOPK]), ALU.mult).then_inc(rt_ready, 1)
                    assert count[0] == TOP_STEPS, count[0]
                    tc = dve.snap(P * tt)
                    dve.wait_ge(rt_tr, l * NB + tt + 1)
                    nc.vector.tensor_copy(ijg[:, :, bass.ds(tc, P)],
                                          ps[:, 6, 0:3 * P].rearrange("k (c t) -> k c t", c=3)).then_inc(rt_ev, 1)
                with dve.Fori(0, T // 16) as r:
                    dve.wait_ge(rt_ev, l * NB + NB)
                    for q in range(4):
                        dve.wait_ge(c_mm, l * 128 + 4 * r + q + 1)
                        for k in range(4):
                            t = 16 * r + 4 * q + k
                            nc.vector.tensor_scalar(oneL[:, 4 * q + k], iota, ijg[:, 0, bass.ds(t, 1)], None,
                                                    ALU.is_equal)
                            ins = nc.vector.tensor_scalar(oneR[:, 4 * q + k], iota, ijg[:, 1, bass.ds(t, 1)],
                                                          ijg[:, 2, bass.ds(t, 1)], ALU.is_equal, ALU.mult)
                        ins.then_inc(lr_done, 1)

                with dve.Fori(0, NKEYS // 4) as r:
                    for s in range(4):
                        j = l * NKEYS + 4 * r + s
                        dve.wait_ge(cf_ready, j + 3)
                        dve.wait_ge(cg_in[s], (l * (NKEYS // 4) + r) * 32 + 32)
                        nc.vector.tensor_tensor(coef[:, s % 2], cg[:, s, 0], cg[:, s, 1], ALU.mult).then_inc(cg_free, 1)
                        dve.wait_ge(tile_done, l * NT + I_W + 4 * r + s + 3)
                        dve.wait_ge(cg_free, l * (NKEYS + 4) + 4 * r + s + 5)
                        nc.vector.tensor_copy(cf_hi[:, s % 2], coef[:, s % 2]).then_inc(cf_hid, 1)
                        dve.wait_ge(cf_hid, j + 1)
                        nc.vector.tensor_tensor(cf_lo[:, s % 2], coef[:, s % 2], cf_hi[:, s % 2].bitcast(F32),
                                                ALU.subtract).then_inc(cf_ready, 1)
                dve.wait_ge(tile_done, (l + 1) * NT + 4)
                for c in range(C):
                    nc.vector.scalar_tensor_tensor(out=xT[:, c], in0=ps[:, c], scalar=md[:, 5 * C + c:5 * C + c + 1],
                                                   in1=xT[:, c], op0=ALU.mult, op1=ALU.add).then_inc(x_upd, 1)
                dve.wait_ge(x_upd, (l + 1) * C)


_OUT = [((1, T, D), "float32")]


def lay_tiles(w):
    return w.reshape(C, P, -1, P).transpose(2, 1, 0, 3)


def kernel(**inputs):
    import concourse.bacc as bacc
    from concourse.bass_utils import run_bass_kernel_spmd as run

    a = {k: np.asarray(v) for k, v in inputs.items()}
    heads = [R * (2 * p + h) + r for p in range(2) for r in range(R) for h in range(2)]
    qcols = np.concatenate([np.arange(HEAD) + HEAD * h for h in heads])
    tiles = []
    for l in range(DEPTH):
        w = a["w_in"][l]
        q, k, v, ga, gb, g1, g2 = np.split(w, np.cumsum([D, 256, 256, D, D, D]), axis=1)
        pair = lambda x, y: np.stack([lay_tiles(x), lay_tiles(y)], 1).reshape(2 * C, P, C, P)
        tiles += [lay_tiles(q[:, qcols]), lay_tiles(k), lay_tiles(v), pair(ga, gb),
                  pair(a["w_o_attn"][l][qcols], g1), pair(a["w_o_conv"][l], g2), lay_tiles(a["w_out"][l]),
                  lay_tiles(a["peer_w_query"][l]),
                  a["peer_u"][l].reshape(P, NKEYS, C, P).transpose(1, 3, 2, 0),
                  a["peer_v"][l].reshape(P, NKEYS, C, P).transpose(1, 0, 2, 3)]
    stream = np.concatenate(tiles)
    chunked = lambda x: x.reshape(DEPTH, -1, P).transpose(2, 0, 1)
    rows = lambda x: np.broadcast_to(x[None], (P,) + x.shape)
    params = np.concatenate([
        chunked(a["norm_mix_g"]), chunked(a["norm_ffn_g"]),
        a["conv_w"].reshape(DEPTH, TAPS, C, P).transpose(3, 0, 2, 1).reshape(P, DEPTH, -1),
        chunked(a["conv_b"]), chunked(a["conv_ln_g"]), chunked(a["conv_ln_b"]),
        np.tile(a["q_norm_g"], (1, 2)).T[:, :, None], np.tile(a["k_norm_g"], (1, 2)).T[:, :, None],
        rows(a["attn_sinks"]), chunked(a["ada_b"])], axis=2)
    arrays = {
        "stream": stream,
        "ada": a["ada_w"].transpose(0, 2, 1).reshape(DEPTH * 6 * C, P, C, P),
        "params_in": params,
        "sub_keys": a["peer_sub_keys"].reshape(DEPTH, 2 * RH, NKEYS, P).transpose(0, 3, 1, 2),
        "constants": constants(),
        "x_in": a["x"][0].T.reshape(C, P, T).transpose(1, 0, 2),
        "c_in": a["c"],
        "pos_in": a["positions"],
    }
    arrays = {k: np.ascontiguousarray(v) for k, v in arrays.items()}
    nc = bacc.Bacc("TRN2", target_bir_lowering=False, num_devices=1)
    aps = [nc.dram_tensor(k, v.shape, mybir.dt.from_np(v.dtype), kind="ExternalInput").ap() for k, v in arrays.items()]
    c_scr = nc.dram_tensor("c_scratch", (NKEYS, P, T), F32).ap()
    g_scr = nc.dram_tensor("gelu_scratch", (NKEYS, P, T), F32).ap()
    out = nc.dram_tensor("trunk_out", (P, C, T), F32, kind="ExternalOutput").ap()
    build_trunk(nc, *aps, c_scr, g_scr, out)
    r = run(nc, [arrays], core_ids=[0])
    y = r.results[0]["trunk_out"]
    return np.ascontiguousarray(y.transpose(1, 0, 2).reshape(D, T).T)[None]
```

```python
from contextlib import ExitStack

import numpy as np
import concourse.bass as bass
from concourse import mybir

F32 = mybir.dt.float32
F32R = mybir.dt.float32r
U32 = mybir.dt.uint32
I32 = mybir.dt.int32
ALU = mybir.AluOpType
ACT = mybir.ActivationFunctionType
AX = mybir.AxisListType.X

P = 128
DEPTH, D, T = 2, 1024, 512
C = D // P
HEAD, NKV, R = 64, 4, 4
NB = T // P
TAPS = 31
PAD = TAPS - 1
NKEYS = 128
RH, TOPK = 8, 16
EPS = 1e-6
LOWEST = -3.0e38
GLU_LATE = 2 * C - 2
EARLY = C // 2
EARLY_TAPS = -(-EARLY * TAPS // (NB * NKV - 2))
FIRST_GATES = 4
RB_TILES = 12
CB_TILES = NKEYS // NB - RB_TILES
ADA_ALL = 6 * C
ADA_1 = 2 * C
ADA_2 = 5 * C
U_C = NB * RB_TILES
LN_STEPS = 2 * C + 2
TOP_STEPS = 145

I_Q, I_K, I_V = 0, 8, 10
I_GLU = 12
I_AG = 28
I_CG = 44
I_OUT = 60
I_QRY = 68
I_U = 84
I_W = I_U + NKEYS
NT = I_W + NKEYS
NE = I_W

O_GN = 0
O_CW = O_GN + 2 * C
O_CB = O_CW + C * TAPS
O_LG = O_CB + C
O_LB = O_LG + C
O_QG = O_LB + C
O_KG = O_QG + 1
O_SK = O_KG + 1
O_AB = O_SK + NKV * R
PL = O_AB + 6 * C

K_ID, K_ONE, K_BLK, K_PERM, K_IOTA, K_M0, K_M1, K_INV, K_EPS = 0, 128, 256, 384, 512, 640, 896, 1152, 1153
NCON = 1154

MAGIC = 12582912.0
PI = float(np.float32(3.1415925))
TP1 = 6.28125
TP2 = float(np.float32(0.00193500518798828125))
TP3 = float(2 * np.pi - TP1 - TP2)


def constants():
    k = np.arange(P)
    con = np.zeros((P, NCON), np.float32)
    con[:, K_ID:K_ID + P] = np.eye(P)
    con[:, K_ONE:K_ONE + P] = 1.0
    con[:, K_BLK:K_BLK + P] = (k[:, None] // HEAD == k[None] // HEAD)
    half = HEAD // 2
    for m in range(P):
        if m % HEAD < half:
            con[m + half, K_PERM + m] = -1.0
        else:
            con[m - half, K_PERM + m] = 1.0
    con[:, K_IOTA:K_IOTA + P] = k[None]
    diff = k[:, None] + P - np.arange(2 * P)[None]
    seen = (diff >= 0) & (diff < P)
    con[:, K_M1:K_M1 + 2 * P] = np.where(seen, 0.0, -1e30)
    con[:, K_M0:K_M0 + 2 * P] = np.where(seen & (np.arange(2 * P)[None] >= P), 0.0, -1e30)
    inv = np.float32(10000.0) ** (-np.arange(0, HEAD, 2, dtype=np.float32) / np.float32(HEAD))
    con[:, K_INV] = inv[k % half]
    con[:, K_EPS] = EPS
    return con


def build_trunk(nc, stream, ada, params_d, keys_d, con_d, x_d, c_d, pos_d, c_scr, g_scr, out_d):
    with ExitStack() as ctx:
        region_base = [nc.sbuf_base]

        def at(name, off_kb, shape, dt=F32):
            return nc.alloc_sbuf_tensor_at(name, shape, dt, offset=off_kb)

        def sem(name):
            return ctx.enter_context(nc.semaphore(name))

        cur = [-(-region_base[0] // 64) * 64]

        def keep(name, shape, dt=F32):
            n = 4
            for d in shape[1:]:
                n *= d
            t = at(name, cur[0], shape, dt)
            cur[0] += -(-n // 64) * 64
            return t

        xT = keep("xT", [P, C, T])
        h_hi = keep("h_hi", [P, C, T], F32R)
        h_lo = keep("h_lo", [P, C, T], F32R)
        raw = keep("raw", [P, 4, C, P])
        w_hi = keep("w_hi", [P, 2, C, P], F32R)
        w_lo = keep("w_lo", [P, 2, C, P], F32R)
        con = keep("con", [P, NCON])
        params = keep("params", [P, DEPTH, PL])
        lp = keep("lp", [P, PL])
        cact = keep("cact", [P, D])
        mv = keep("mv", [P, 3 * C])
        md = keep("md", [P, 6 * C])
        gs = keep("gs", [P, 2, C])
        macc = keep("macc", [P, 4])
        spare = keep("spare", [P, 16])
        st4 = keep("st4", [P, 6, R])
        cosT = keep("cosT", [P, T])
        sinT = keep("sinT", [P, T])
        rstd = keep("rstd", [P, T])
        sq = keep("sq", [P, 2, T])
        hx = keep("hx", [P, 2, T])
        hs = keep("hs", [P, 2, T])
        sg = keep("sg", [P, 2, T])
        cur[0] = -(-cur[0] // 64) * 64
        base = cur[0]
        KB = 1024
        assert base + 91 * KB <= nc.sbuf_usable_end, (base, nc.sbuf_usable_end)
        o_hi = at("o_hi", base, [P, C, T], F32R)
        o_lo = at("o_lo", base + 16 * KB, [P, C, T], F32R)
        qT = at("qT", base + 32 * KB, [P, C, T])
        kT = at("kT", base + 48 * KB, [P, 2, P + T])
        vn = at("vn", base + 53 * KB, [P, NB + 1, NKV * HEAD])
        uT = at("uT", base + 58 * KB, [P, C, PAD + T])
        n_hi = at("n_hi", base + 58 * KB, [P, C, T], F32R)
        yT = at("yT", base + 75 * KB, [P, C, T])
        n_lo = at("n_lo", base + 75 * KB, [P, C, T], F32R)
        vT = at("vT", base + 75 * KB, [P, 2, T])
        scores_sb = [at("sc", base + 83 * KB, [P, R, 2 * P]), hs[:].rearrange("p a (b k) -> p (a b) k", b=2)]
        pT = at("pT", base + 87 * KB, [P, 2, R, P])
        turns = at("turns", base + 14 * KB, [P, T])
        rows0 = at("rows0", base + 16 * KB, [P, ADA_1, D])
        pos_i = at("pos_i", base + 8 * KB, [P, T], I32)
        ang = at("ang", base + 10 * KB, [P, T])
        turn = at("turn", base + 12 * KB, [P, T])
        rows = [at(f"rows{k + 1}", base + kb * KB, [P, D]) for k, kb in enumerate((28, 79, 83, 87))]
        cgate = at("cgate", base + 48 * KB, [P, FIRST_GATES, T])
        S_all = at("S_all", base, [P, NB, 2 * RH, NKEYS])
        qk = at("qk", base + 32 * KB, [P, 2 * RH, T])
        s_w = at("s_w", base + 32 * KB, [P, 2 * RH, NKEYS])
        eq = at("eq", base + 32 * KB, [P, RH * TOPK, TOPK])
        cand = at("cand", base + 40 * KB, [P, RH, TOPK * TOPK])
        small = base + 48 * KB
        v16 = at("v16", small, [P, 2 * RH, TOPK])
        i16 = at("i16", small + 1024, [P, 2 * RH, TOPK], U32)
        i16f = at("i16f", small + 2048, [P, 2 * RH, TOPK])
        t16 = at("t16", small + 3072, [P, RH, TOPK])
        p16 = at("p16", small + 3584, [P, RH, TOPK], U32)
        ab = at("ab", small + 4096, [P, 2, RH * TOPK], U32)
        abf = at("abf", small + 5120, [P, 2, RH * TOPK])
        routed = at("routed", small + 6144, [P, 3, RH * TOPK])
        esum = at("esum", small + 7680, [P, 2, RH])
        ijg = at("ijg", base + 64 * KB, [P, 3, T])
        g_out = at("g_out", base + 70 * KB, [P, 2, T])
        stage = at("stage", base, [P, NKEYS, P])
        keys = at("keys", base + 74 * KB, [P, 2 * RH, NKEYS])
        oneL = at("oneL", base + 74 * KB, [P, 16, P])
        oneR = at("oneR", base + 82 * KB, [P, 16, P])
        cg = at("cg", base, [P, 4, 2, T])
        coef = at("coef", base + 16 * KB, [P, 2, T])
        cf_hi = at("cf_hi", base + 20 * KB, [P, 2, T], F32R)
        cf_lo = at("cf_lo", base + 24 * KB, [P, 2, T], F32R)

        ps = ctx.enter_context(nc.psum_tensor("ps", [P, 8, 512], F32))
        ident = con[:, K_ID:K_ID + P]
        ones = con[:, K_ONE:K_ONE + P]
        eps = con[:, K_EPS:K_EPS + 1]
        iota = con[:, K_IOTA:K_IOTA + P]

        loaded = [sem(f"tile_loaded{s}") for s in range(4)]
        hi_done = sem("hi_done")
        lo_done = sem("lo_done")
        tile_done = sem("tile_done")
        bank_read = [sem(f"bank_read{b}") for b in range(2)]
        primed = sem("primed")
        const_in = sem("const_in")
        x_in = sem("x_in")
        ada_in = [sem(f"ada_in{s}") for s in range(4)]
        c_silu = sem("c_silu")
        mod_step = sem("mod_step")
        mod_add = sem("mod_add")
        mod_sum = sem("mod_sum")
        rope_step = sem("rope_step")
        rope_sin = sem("rope_sin")
        lay = sem("lay")
        x_upd = sem("x_upd")
        sq_done = sem("sq_done")
        sq_used = sem("sq_used")
        rt_done = sem("rt_done")
        rs_done = sem("rs_done")
        hx_done = sem("hx_done")
        hs_done = sem("hs_done")
        hhi_done = sem("hhi_done")
        h_ready = sem("h_ready")
        qsq = sem("qsq")
        qss = sem("qss")
        qrt = sem("qrt")
        qrs = sem("qrs")
        qn = sem("qn")
        rot = sem("rot")
        qa = sem("qa")
        qcos = sem("qcos")
        qrope = sem("qrope")
        pad0 = sem("pad0")
        v_tr = sem("v_tr")
        v_ev = sem("v_ev")
        s_mm = sem("s_mm")
        s_msk = sem("s_msk")
        a_max = sem("a_max")
        a_neg = sem("a_neg")
        a_exp = sem("a_exp")
        a_den = sem("a_den")
        a_nrm = sem("a_nrm")
        p_tr = sem("p_tr")
        p_ev = sem("p_ev")
        o_mm = sem("o_mm")
        o_hid = sem("o_hid")
        o_lod = sem("o_lod")
        conv_step = sem("conv_step")
        ln_mm = sem("ln_mm")
        ln_step = sem("ln_step")
        ln_sq = sem("ln_sq")
        ln_silu = sem("ln_silu")
        ln_hi = sem("ln_hi")
        ln_lo = sem("ln_lo")
        mrg = sem("mrg")
        mrg_hi = sem("mrg_hi")
        mrg_lo = sem("mrg_lo")
        key_in = sem("key_in")
        r_mm = sem("r_mm")
        r_ev = sem("r_ev")
        top_step = sem("top_step")
        g_exp = sem("g_exp")
        rt_ready = sem("rt_ready")
        rt_tr = sem("rt_tr")
        rt_ev = sem("rt_ev")
        g_st = [sem(f"gelu_stored{s}") for s in range(2)]
        lr_done = sem("lr_done")
        c_mm = sem("c_mm")
        c_ev = sem("c_ev")
        c_st = sem("c_stored")
        cg_in = [sem(f"cg_in{s}") for s in range(4)]
        cg_free = sem("cg_free")
        cf_hid = sem("cf_hid")
        cf_ready = sem("cf_ready")
        out_st = sem("out_st")

        block = ctx.enter_context(nc.Block())

        @block.sync
        def _(sp):
            sp.dma_start(con[:], con_d).then_inc(const_in, 16)
            sp.dma_start(params[:], params_d).then_inc(const_in, 16)
            sp.dma_start(cact[:], c_d.broadcast_to([P, D])).then_inc(const_in, 16)
            sp.dma_start(pos_i[:], pos_d.broadcast_to([P, T])).then_inc(const_in, 16)
            for n in range(ADA_1):
                sp.dma_start(rows0[:, n], ada[n]).then_inc(ada_in[n // 4], 16)
                if n == 7:
                    sp.dma_start(xT[:], x_d).then_inc(x_in, 16)
            sp.wait_ge(primed, 1)

            with sp.Fori(0, DEPTH) as l:
                def load(s, g):
                    n = sp.snap(g)
                    sp.wait_ge(lo_done, n + 1)
                    sp.dma_start(raw[:, s], stream[n]).then_inc(loaded[s], 16)

                def load_rows(s, g, used):
                    n = sp.snap(g)
                    sp.wait_ge(mod_step, used)
                    sp.dma_start(rows[s][:], ada[n]).then_inc(ada_in[s], 16)

                for i in range(20):
                    load(i % 4, l * NT + i)
                    if i == 3:
                        for s in range(4):
                            load_rows(s, l * ADA_ALL + ADA_1 + s, l * ADA_ALL + ADA_1 + 1)
                    if i >= 8 and 2 * (i - 6) < ADA_2 - ADA_1:
                        for n in range(ADA_1 + 2 * (i - 6), ADA_1 + 2 * (i - 6) + 2):
                            load_rows(n % 4, l * ADA_ALL + n, l * ADA_ALL + n - 2)
                with sp.Fori(20 // 4, I_W // 4) as r:
                    for s in range(4):
                        load(s, l * NT + 4 * r + s)
                for s in range(4):
                    load(s, l * NT + I_W + s)
                def load_cg(s, j, k):
                    jj = sp.snap(j)
                    sp.wait_ge(cg_free, k)
                    sp.dma_start(cg[:, s, 0].rearrange("i (b t) -> i b t", b=NB),
                                 c_scr[:, :, bass.ds(jj, 1)].rearrange("b i o t -> i (b o) t")).then_inc(cg_in[s], 16)
                    sp.dma_start(cg[:, s, 1], g_scr[jj]).then_inc(cg_in[s], 16)

                with sp.Fori(0, 3 * C // 4) as r:
                    for s in range(4):
                        load_cg(s, 4 * r + s, l * (NKEYS + 4) + 4 * r + s + 1)
                        n = ADA_2 + s
                        load_rows(s, l * ADA_ALL + n + 4 * r, l * ADA_ALL + n - 2 + 4 * r)
                        load(s, l * NT + I_W + 4 * r + s + 4)
                with sp.Fori(3 * C // 4, NKEYS // 4 - 1) as r:
                    for s in range(4):
                        load_cg(s, 4 * r + s, l * (NKEYS + 4) + 4 * r + s + 1)
                        load(s, l * NT + I_W + 4 * r + s + 4)
                for s in range(4):
                    load_cg(s, NKEYS - 4 + s, l * (NKEYS + 4) + NKEYS - 4 + s + 1)

            sp.wait_ge(x_upd, DEPTH * C)
            sp.dma_start(out_d, xT[:]).then_inc(out_st, 16)
            sp.wait_ge(out_st, 16)

        @block.gpsimd
        def _(pool):
            nc.gpsimd.memset(spare[:, 15:16], 0.0).then_inc(lo_done, 4)
            with pool.Fori(0, DEPTH) as l:
                def low(s, g):
                    through, high = pool.snap(g + 3), pool.snap(g + 1)
                    pool.wait_ge(tile_done, through)
                    pool.wait_ge(hi_done, high)
                    nc.gpsimd.tensor_tensor(w_lo[:, s % 2], raw[:, s], w_hi[:, s % 2].bitcast(F32),
                                            ALU.subtract).then_inc(lo_done, 1)

                def h_low(w):
                    for c in range(C):
                        n = (2 * l + w) * C + c + 1
                        pool.wait_ge(hhi_done, n)
                        nc.gpsimd.tensor_tensor(h_lo[:, c], hs[:, c % 2], h_hi[:, c].bitcast(F32),
                                                ALU.subtract).then_inc(h_ready, 1)

                for i in range(2):
                    low(i, l * NT + i)
                h_low(0)
                nc.gpsimd.memset(kT[:, :, 0:P], 0.0).then_inc(pad0, 1)
                nc.gpsimd.memset(vn[:, 0], 0.0).then_inc(pad0, 1)
                nc.gpsimd.memset(uT[:, :, 0:PAD], 0.0).then_inc(pad0, 1)
                for i in range(2, 4):
                    low(i, l * NT + i)
                with pool.Fori(1, I_CG // 4) as r:
                    for s in range(4):
                        low(s, l * NT + 4 * r + s)
                for i in range(I_CG, I_CG + FIRST_GATES + 2):
                    low(i % 4, l * NT + i)
                for c in range(C):
                    pool.wait_ge(ln_hi, l * C + c + 1)
                    nc.gpsimd.tensor_tensor(n_lo[:, c], hs[:, c % 2], n_hi[:, c].bitcast(F32),
                                            ALU.subtract).then_inc(ln_lo, 1)
                for m in range(C):
                    first = I_CG + FIRST_GATES + m + 2 if m < FIRST_GATES else I_CG + 2 * m + 2
                    for i in range(first, first + (1 if m < FIRST_GATES else 2)):
                        low(i % 4, l * NT + i)
                    pool.wait_ge(mrg_hi, l * C + m + 1)
                    nc.gpsimd.tensor_tensor(o_lo[:, m], hx[:, m % 2], o_hi[:, m].bitcast(F32),
                                            ALU.subtract).then_inc(mrg_lo, 1)
                for i in range(I_OUT + 2, I_QRY + 2):
                    low(i % 4, l * NT + i)
                h_low(1)
                for i in range(I_QRY + 2, I_QRY + 4):
                    low(i % 4, l * NT + i)
                with pool.Fori(I_QRY // 4 + 1, NT // 4) as r:
                    for s in range(4):
                        low(s, l * NT + 4 * r + s)

        @block.tensor
        def _(pe):
            pe.wait_ge(const_in, 64)
            with pe.Fori(0, DEPTH) as l:
                def read_no(i):
                    return l * (NE // 2) + i // 2 + 2

                def product(s, g, e, hi, lo, ready=None, chunks=None):
                    b = s % 2
                    if ready is not None:
                        pe.wait_ge(*ready)
                    pe.wait_ge(bank_read[b], e)
                    pe.wait_ge(lo_done, g + 5)
                    for c in range(C):
                        wh, wl = w_hi[:, b, c], w_lo[:, b, c]
                        if chunks is not None:
                            pe.wait_ge(chunks[0], chunks[1] + c + 1)
                        nc.tensor.matmul(ps[:, b], wh, hi[:, c], start=c == 0, stop=False)
                        nc.tensor.matmul(ps[:, b], wh, lo[:, c], start=False, stop=False)
                        mm = nc.tensor.matmul(ps[:, b], wl, hi[:, c], start=False, stop=c == C - 1)
                    mm.then_inc(tile_done, 1)

                def proj(i, hi, lo, chunks=None):
                    product(i % 4, l * NT + i, l * (NE // 2) + i // 2 + 1, hi, lo, chunks=chunks)

                def proj_loop(i0, i1, hi, lo, ready=None):
                    with pe.Fori(i0 // 4, i1 // 4) as r:
                        for s in range(4):
                            product(s, l * NT + 4 * r + s, l * (NE // 2) + 2 * r + s // 2 + 1, hi, lo,
                                    ready if s == 0 else None)

                def norm_sums(w):
                    for c in range(C):
                        pe.wait_ge(sq_done, (2 * l + w) * C + c + 1)
                        nc.tensor.matmul(ps[:, 7], ones, sq[:, c % 2], start=c == 0,
                                         stop=c == C - 1).then_inc(sq_used, 1)

                norm_sums(0)

                def rms_sum(k):
                    pe.wait_ge(qsq, l * 10 + k + 1)
                    if k >= 1:
                        pe.wait_ge(qrt, l * 10 + k)
                    nc.tensor.matmul(ps[:, 7], con[:, K_BLK:K_BLK + P], sq[:, k % 2],
                                     start=True, stop=True).then_inc(qss, 1)

                def rotate(k):
                    pe.wait_ge(qn, l * 10 + k + 1)
                    if k >= 1:
                        pe.wait_ge(qa, l * 10 + k)
                    nc.tensor.matmul(ps[:, 6], con[:, K_PERM:K_PERM + P], hx[:, k % 2],
                                     start=True, stop=True).then_inc(rot, 1)

                for i in range(I_GLU + 2):
                    proj(i, h_hi, h_lo, (h_ready, 2 * l * C) if i == 0 else None)
                    if 1 <= i <= 10:
                        rms_sum(i - 1)
                    if 3 <= i <= 12:
                        rotate(i - 3)
                pe.wait_ge(bank_read[1], read_no(I_GLU - 1))
                for n in range(NB):
                    if n >= 1:
                        pe.wait_ge(v_ev, l * NB + n)
                    for p in range(2):
                        mm = nc.tensor.transpose(ps[:, 2, p * P:(p + 1) * P], vT[:, p, n * P:(n + 1) * P], ident)
                    mm.then_inc(v_tr, 1)

                units = [(n, g) for n in range(NB) for g in range(NKV)]

                def scores(u):
                    n, g = units[u]
                    p, lo64 = g // 2, (g % 2) * HEAD
                    if u >= 1:
                        pe.wait_ge(s_msk, l * 16 + u)
                    for r in range(R):
                        mm = nc.tensor.matmul(ps[:, 2 + r // 2, (r % 2) * 256:(r % 2) * 256 + 256],
                                              qT[lo64:lo64 + HEAD, p * R + r, n * P:(n + 1) * P],
                                              kT[lo64:lo64 + HEAD, p, n * P:(n + 2) * P],
                                              start=True, stop=True)
                    mm.then_inc(s_mm, 1)

                def values(u):
                    n, g = units[u]
                    lo64 = (g % 2) * HEAD
                    pe.wait_ge(a_nrm, l * 16 + u + 1)
                    if u >= 1:
                        pe.wait_ge(p_ev, l * 32 + 2 * u)
                    for kb in range(2):
                        for r in range(R):
                            mm = nc.tensor.transpose(ps[:, 4 + kb, r * P:(r + 1) * P],
                                                     scores_sb[u % 2][:, r, kb * P:(kb + 1) * P], ident)
                        mm.then_inc(p_tr, 1)
                    if u >= 1:
                        pe.wait_ge(o_lod, l * 16 + u)
                    for kb in range(2):
                        pe.wait_ge(p_ev, l * 32 + 2 * u + kb + 1)
                        mm = nc.tensor.matmul(ps[lo64:lo64 + HEAD, 6], vn[:, n + kb, g * HEAD:(g + 1) * HEAD],
                                              pT[:, kb].rearrange("k r q -> k (r q)"),
                                              start=kb == 0, stop=kb == 1)
                    mm.then_inc(o_mm, 1)

                pe.wait_ge(qrope, l * 10 + 10)
                pe.wait_ge(v_ev, l * NB + NB)
                pe.wait_ge(pad0, 3 * l + 3)
                scores(0)
                for u in range(len(units)):
                    if u + 1 < len(units):
                        scores(u + 1)
                    if u < GLU_LATE:
                        proj(I_GLU + 2 + u, h_hi, h_lo)
                    values(u)
                def pairs(i0, n, hi, lo, ready):
                    with pe.Fori(i0 // 4, i0 // 4 + n // 2) as r:
                        for s in range(4):
                            a, b = (h_hi, h_lo) if s % 2 == 0 else (hi, lo)
                            product(s, l * NT + 4 * r + s, l * (NE // 2) + 2 * r + s // 2 + 1, a, b,
                                    ready if s % 2 == 1 else None)

                def channel_sum(c):
                    pe.wait_ge(conv_step, l * C * TAPS + (c // 2 + 1) * 2 * TAPS)
                    nc.tensor.matmul(ps[:, 7], ones, yT[:, c], start=c == 0, stop=c == C - 1).then_inc(ln_mm, 1)

                for c in range(EARLY):
                    channel_sum(c)
                pairs(I_AG, C, o_hi, o_lo, (o_lod, l * 16 + 16))
                proj(I_CG, h_hi, h_lo)
                for c in range(EARLY, C):
                    channel_sum(c)
                proj(I_CG + 1, h_hi, h_lo)
                proj(I_CG + 2, h_hi, h_lo)
                for c in range(C):
                    pe.wait_ge(ln_sq, l * C + c + 1)
                    nc.tensor.matmul(ps[:, 6], ones, sq[:, c % 2], start=c == 0, stop=c == C - 1).then_inc(ln_mm, 1)
                for i in range(I_CG + 3, I_CG + FIRST_GATES):
                    proj(i, h_hi, h_lo)
                for m in range(FIRST_GATES):
                    proj(I_CG + FIRST_GATES + m, n_hi, n_lo, (ln_lo, l * C) if m == 0 else None)
                pairs(I_CG + 2 * FIRST_GATES, C - FIRST_GATES, n_hi, n_lo, None)
                for s in range(4):
                    proj(I_OUT + s, o_hi, o_lo, (mrg_lo, l * C) if s == 0 else None)
                proj_loop(I_OUT + 4, I_QRY, o_hi, o_lo)
                norm_sums(1)
                for s in range(4):
                    proj(I_QRY + s, h_hi, h_lo, (h_ready, 2 * l * C + C) if s == 0 else None)
                proj_loop(I_QRY + 4, I_U, h_hi, h_lo)
                pe.wait_ge(key_in, 16 * l + 16)
                for b in range(2):
                    pe.wait_ge(bank_read[b], read_no(I_U - 2 + b))
                for tt in range(NB):
                    for q in range(4):
                        if tt >= 1:
                            pe.wait_ge(r_ev, l * 16 + (tt - 1) * 4 + q + 1)
                        for k in range(4):
                            hp = 4 * q + k
                            mm = nc.tensor.matmul(ps[:, 2 + q, k * P:(k + 1) * P], qk[:, hp, tt * P:(tt + 1) * P],
                                                  keys[:, hp], start=True, stop=True)
                        mm.then_inc(r_mm, 1)
                with pe.Fori(0, NB) as tt:
                    with pe.Fori(0, RB_TILES // 4) as r:
                        for s in range(4):
                            product(s, l * NT + I_U + RB_TILES * tt + 4 * r + s,
                                    l * (NE // 2) + I_U // 2 + RB_TILES // 2 * tt + 2 * r + s // 2 + 1, h_hi, h_lo)
                    pe.wait_ge(rt_ready, l * NB + tt + 1)
                    for k in range(3):
                        mm = nc.tensor.transpose(ps[:, 6, k * P:(k + 1) * P], routed[:, k], ident)
                    mm.then_inc(rt_tr, 1)
                with pe.Fori(0, NB) as tb:
                    with pe.Fori(0, 2) as r:
                        for s in range(4):
                            product(s, l * NT + I_U + U_C + CB_TILES * tb + 4 * r + s,
                                    l * (NE // 2) + (I_U + U_C) // 2 + CB_TILES // 2 * tb + 2 * r + s // 2 + 1,
                                    h_hi, h_lo)
                            for q in range(4):
                                n4 = l * 128 + 32 * tb + 16 * r + 4 * s + q
                                pe.wait_ge(c_ev, n4 + 1)
                                pe.wait_ge(lr_done, n4 + 1)
                                for k in range(4):
                                    mm = nc.tensor.matmul(ps[:, 2 + q, k * P:(k + 1) * P], oneL[:, 4 * q + k],
                                                          oneR[:, 4 * q + k], start=True, stop=True)
                                mm.then_inc(c_mm, 1)
                    with pe.Fori(2, CB_TILES // 4) as r:
                        for s in range(4):
                            product(s, l * NT + I_U + U_C + CB_TILES * tb + 4 * r + s,
                                    l * (NE // 2) + (I_U + U_C) // 2 + CB_TILES // 2 * tb + 2 * r + s // 2 + 1,
                                    h_hi, h_lo)

                def experts(s, j, g, first, last):
                    b = s % 2
                    pe.wait_ge(cf_ready, j + 5)
                    pe.wait_ge(lo_done, g + 5)
                    for c in range(C):
                        nc.tensor.matmul(ps[:, c], w_hi[:, b, c], cf_hi[:, b], start=first, stop=False)
                        nc.tensor.matmul(ps[:, c], w_hi[:, b, c], cf_lo[:, b], start=False, stop=False)
                        mm = nc.tensor.matmul(ps[:, c], w_lo[:, b, c], cf_hi[:, b], start=False, stop=last)
                    mm.then_inc(tile_done, 1)

                for b in range(2):
                    pe.wait_ge(bank_read[b], (l + 1) * (NE // 2) + 1)
                pe.wait_ge(c_ev, (l + 1) * 128 + 4)
                pe.wait_ge(rt_ev, (l + 1) * NB)
                for s in range(4):
                    experts(s, l * NKEYS + s, l * NT + I_W + s, s == 0, False)
                with pe.Fori(1, NKEYS // 4 - 1) as r:
                    for s in range(4):
                        experts(s, l * NKEYS + 4 * r + s, l * NT + I_W + 4 * r + s, False, False)
                for s in range(4):
                    j = NKEYS - 4 + s
                    experts(s, l * NKEYS + j, l * NT + I_W + j, False, s == 3)

        @block.scalar
        def _(act):
            act.wait_ge(const_in, 64)
            nc.scalar.activation(cact[:], cact[:], ACT.Silu).then_inc(c_silu, 1)
            for k, dst in enumerate((sinT, cosT)):
                act.wait_ge(rope_sin, 2 * k + 1)
                nc.scalar.activation(dst[:], turn[:], ACT.Sin).then_inc(rope_sin, 1)
            act.wait_ge(primed, 1)
            act.wait_ge(x_in, 16)
            with act.Fori(0, DEPTH) as l:
                def read_no(i):
                    return l * (NE // 2) + i // 2 + 2

                def high(s, g):
                    act.wait_ge(tile_done, g + 3)
                    nc.scalar.copy(w_hi[:, s % 2], raw[:, s]).then_inc(hi_done, 1)

                def high_at(i):
                    act.wait_ge(loaded[i % 4], (l * (NT // 4) + i // 4 + 1) * 16)
                    high(i % 4, l * NT + i)

                def high_in(s, i0, r):
                    act.wait_ge(loaded[s], (l * (NT // 4) + r + i0 // 4 + 1) * 16)
                    high(s, l * NT + i0 + 4 * r)

                def norm(w):
                    for c in range(C):
                        n = (2 * l + w) * C + c
                        if w == 1:
                            act.wait_ge(bank_read[c % 2], read_no(I_OUT + c))
                        if c >= 2:
                            act.wait_ge(sq_used, (2 * l + w) * C + c - 1)
                        nc.scalar.activation(sq[:, c % 2], xT[:, c], ACT.Square).then_inc(sq_done, 1)
                    act.wait_ge(lay, 3 * l + w + 2)
                    act.wait_ge(sq_used, (2 * l + w) * C + C)
                    nc.scalar.activation(rstd[:], ps[:, 7], ACT.Sqrt, scale=1.0 / D, bias=eps).then_inc(rt_done, 1)
                    for c in range(C):
                        n = (2 * l + w) * C + c
                        act.wait_ge(hx_done, n + 1)
                        if c >= 2:
                            act.wait_ge(h_ready, (2 * l + w) * C + c - 1)
                        nc.scalar.activation(hs[:, c % 2], hx[:, c % 2], ACT.Identity, scale=gs[:, w, c:c + 1],
                                             bias=md[:, 3 * w * C + c:3 * w * C + c + 1]).then_inc(hs_done, 1)
                        act.wait_ge(hs_done, n + 1)
                        nc.scalar.copy(h_hi[:, c], hs[:, c % 2]).then_inc(hhi_done, 1)

                high_at(0)
                high_at(1)
                act.wait_ge(lay, 3 * l + 1)
                norm(0)

                def q_root(k):
                    act.wait_ge(qss, l * 10 + k + 1)
                    if k >= 2:
                        act.wait_ge(qn, l * 10 + k - 1)
                    nc.scalar.activation(hs[:, k % 2], ps[:, 7], ACT.Sqrt, scale=1.0 / HEAD, bias=eps).then_inc(qrt, 1)

                for i in range(I_GLU):
                    high_at(i + 2)
                    act.wait_ge(tile_done, l * NT + i + 5)
                    dst = qT[:, i] if i < I_K else kT[:, i - I_K, P:P + T] if i < I_V else vT[:, i - I_V]
                    nc.scalar.copy(dst, ps[:, i % 2]).then_inc(bank_read[i % 2], 1)
                    if i < I_V:
                        if i >= 2:
                            act.wait_ge(qss, l * 10 + i - 1)
                        act.wait_ge(bank_read[i % 2], read_no(i))
                        nc.scalar.activation(sq[:, i % 2], dst, ACT.Square).then_inc(qsq, 1)
                    if 1 <= i <= 10:
                        q_root(i - 1)

                def sigmoid(s, i):
                    act.wait_ge(bank_read[1], read_no(i - 3))
                    act.wait_ge(tile_done, l * NT + i + 5)
                    nc.scalar.activation(sg[:, (s // 2) % 2], ps[:, 0], ACT.Sigmoid).then_inc(bank_read[0], 1)

                def sigmoid_in(s, i0, r):
                    act.wait_ge(bank_read[1], l * (NE // 2) + (i0 + s - 3) // 2 + 2 * r + 2)
                    act.wait_ge(tile_done, l * NT + i0 + s + 4 * r + 5)
                    nc.scalar.activation(sg[:, s // 2], ps[:, 0], ACT.Sigmoid).then_inc(bank_read[0], 1)

                act.wait_ge(qrope, l * 10 + 10)
                def glu_tile(i):
                    if i % 2 == 0:
                        sigmoid(i - I_GLU, i)
                    high_at(i + 2)

                def probs(u):
                    sc = scores_sb[u % 2]
                    act.wait_ge(a_den, 3 * (l * 16 + u) + 1)
                    act.wait_ge(a_neg, l * 16 + u + 1)
                    for r in range(R):
                        nc.scalar.activation(sc[:, r], sc[:, r], ACT.Exp, bias=st4[:, 1, r:r + 1],
                                             accum_out=st4[:, 2, r:r + 1])
                    nc.scalar.activation(st4[:, 4], st4[:, 3], ACT.Exp).then_inc(a_exp, 1)

                glu_tile(I_GLU)
                glu_tile(I_GLU + 1)
                probs(0)
                for u in range(16):
                    n, g = u // NKV, u % NKV
                    p, lo64 = g // 2, (g % 2) * HEAD
                    if u < 15:
                        probs(u + 1)
                    act.wait_ge(p_tr, l * 32 + 2 * u + 1)
                    if u >= 1:
                        act.wait_ge(o_mm, l * 16 + u)
                    nc.scalar.copy(pT[:, 0], ps[:, 4].rearrange("k (r q) -> k r q", r=R)).then_inc(p_ev, 1)
                    act.wait_ge(p_tr, l * 32 + 2 * u + 2)
                    nc.scalar.copy(pT[:, 1], ps[:, 5].rearrange("k (r q) -> k r q", r=R)).then_inc(p_ev, 1)
                    if u < GLU_LATE:
                        glu_tile(I_GLU + 2 + u)
                    act.wait_ge(o_mm, l * 16 + u + 1)
                    nc.scalar.copy(o_hi[lo64:lo64 + HEAD, p * R:(p + 1) * R, n * P:(n + 1) * P],
                                   ps[lo64:lo64 + HEAD, 6].rearrange("f (r q) -> f r q", r=R)).then_inc(o_hid, 1)
                with act.Fori(0, 4) as r:
                    for s in range(4):
                        if s % 2 == 0:
                            sigmoid_in(s, I_AG, r)
                        high_in((s + 2) % 4, I_AG + s + 2, r)
                def first_gate(m):
                    high_at(I_CG + m + 2)
                    act.wait_ge(tile_done, l * NT + I_CG + m + 5)
                    nc.scalar.activation(cgate[:, m], ps[:, m % 2], ACT.Sigmoid).then_inc(bank_read[m % 2], 1)

                def centred_square(c):
                    act.wait_ge(ln_step, l * LN_STEPS + 1 + c + 1)
                    if c >= 2:
                        act.wait_ge(ln_mm, l * 2 * C + C + c - 1)
                    nc.scalar.activation(sq[:, c % 2], yT[:, c], ACT.Square).then_inc(ln_sq, 1)

                first_gate(0)
                centred_square(0)
                centred_square(1)
                first_gate(1)
                first_gate(2)
                for c in range(2, C):
                    centred_square(c)
                for m in range(3, FIRST_GATES):
                    first_gate(m)
                act.wait_ge(ln_mm, l * 2 * C + 2 * C)
                nc.scalar.activation(rstd[:], ps[:, 6], ACT.Sqrt, scale=1.0 / D, bias=eps).then_inc(ln_silu, 1)
                for c in range(C):
                    act.wait_ge(ln_step, l * LN_STEPS + C + 2 + c + 1)
                    if c >= 2:
                        act.wait_ge(ln_lo, l * C + c - 1)
                    nc.scalar.activation(hs[:, c % 2], hx[:, c % 2], ACT.Silu, scale=lp[:, O_LG + c:O_LG + c + 1],
                                         bias=lp[:, O_LB + c:O_LB + c + 1]).then_inc(ln_silu, 1)
                    act.wait_ge(ln_silu, l * (C + 1) + 1 + c + 1)
                    nc.scalar.copy(n_hi[:, c], hs[:, c % 2]).then_inc(ln_hi, 1)
                for m in range(C):
                    if m < FIRST_GATES:
                        high_at(I_CG + FIRST_GATES + m + 2)
                    else:
                        i = I_CG + 2 * m
                        sigmoid(2 * (m % 2), i)
                        high_at(i + 2)
                        high_at(i + 3)
                    act.wait_ge(mrg, l * C + m + 1)
                    nc.scalar.copy(o_hi[:, m], hx[:, m % 2]).then_inc(mrg_hi, 1)
                for i in range(I_OUT, I_QRY):
                    high_at(i + 2)
                norm(1)
                ll = act.snap(l + 0)
                act.wait_ge(bank_read[1], read_no(I_QRY - 1))
                act.dma_start(keys[:], keys_d[ll]).then_inc(key_in, 16)
                for i in range(I_QRY, I_U):
                    high_at(i + 2)
                    act.wait_ge(tile_done, l * NT + i + 5)
                    nc.scalar.copy(qk[:, i - I_QRY], ps[:, i % 2]).then_inc(bank_read[i % 2], 1)
                for n in range(16):
                    act.wait_ge(r_mm, l * 16 + n + 1)
                    nc.scalar.copy(S_all[:, n // 4, 4 * (n % 4):4 * (n % 4) + 4],
                                   ps[:, 2 + n % 4].rearrange("t (k n) -> t k n", k=4)).then_inc(r_ev, 1)

                def gelu(s, j, nth, g):
                    jj = act.snap(j)
                    act.wait_ge(g_st[s % 2], (l * (NKEYS // 2) + nth) * 16 + 16)
                    act.wait_ge(tile_done, g + 5)
                    nc.scalar.activation(g_out[:, s % 2], ps[:, s % 2], ACT.Gelu).then_inc(bank_read[s % 2], 1)
                    act.wait_ge(bank_read[s % 2], l * (NE // 2) + I_U // 2 + nth + 2)
                    act.dma_start(g_scr[jj], g_out[:, s % 2]).then_inc(g_st[s % 2], 16)

                def u_tile(s, i, r, nth):
                    high_in((s + 2) % 4, I_U + i + s + 2, r)
                    gelu(s, i + 4 * r + s, nth + s // 2, l * NT + I_U + i + 4 * r + s)

                with act.Fori(0, NB) as tt:
                    with act.Fori(0, RB_TILES // 4 - 1) as r:
                        for s in range(4):
                            u_tile(s, 0, RB_TILES // 4 * tt + r, RB_TILES // 2 * tt + 2 * r)
                    act.wait_ge(g_exp, 2 * (l * NB + tt) + 1)
                    nc.scalar.activation(t16[:], t16[:], ACT.Exp).then_inc(g_exp, 1)
                    for s in range(4):
                        u_tile(s, RB_TILES - 4, RB_TILES // 4 * tt, RB_TILES // 2 * tt + RB_TILES // 2 - 2)
                with act.Fori(0, NB) as tb:
                    with act.Fori(0, 2) as r:
                        for s in range(4):
                            u_tile(s, U_C, CB_TILES // 4 * tb + r, U_C // 2 + CB_TILES // 2 * tb + 2 * r)
                            if s == 0:
                                act.wait_ge(c_st, (l * NB + tb) * 64 + 64)
                            for q in range(4):
                                t0 = act.snap(64 * r + 16 * s + 4 * q)
                                act.wait_ge(c_mm, l * 128 + 32 * tb + 16 * r + 4 * s + q + 5)
                                nc.scalar.copy(stage[:, :, bass.ds(t0, 4)].rearrange("i j t -> i t j"),
                                               ps[:, 2 + q].rearrange("i (t j) -> i t j", t=4)).then_inc(c_ev, 1)
                    tb0 = act.snap(tb + 0)
                    act.wait_ge(c_ev, l * 128 + 32 * tb + 32 + 4)
                    for k in range(4):
                        act.dma_start(c_scr[bass.ds(tb0, 1), :, 32 * k:32 * k + 32].rearrange("b i j t -> i (b j) t"),
                                      stage[:, 32 * k:32 * k + 32]).then_inc(c_st, 16)
                    with act.Fori(2, CB_TILES // 4) as r:
                        for s in range(4):
                            u_tile(s, U_C, CB_TILES // 4 * tb + r, U_C // 2 + CB_TILES // 2 * tb + 2 * r)
                for b in range(2):
                    act.wait_ge(g_st[b], (l + 1) * (NKEYS // 2 * 16) + 16)
                act.wait_ge(c_st, (l + 1) * (NB * 64) + 64)
                nc.scalar.copy(st4[:, 4], st4[:, 3]).then_inc(cg_free, 4)
                for i in range(I_W + 2, I_W + 4):
                    high_at(i)
                with act.Fori(0, NKEYS // 4 - 1) as r:
                    for s in range(4):
                        high_in(s, I_W + 4 + s, r)

        @block.vector
        def _(dve):
            starts = [(bank_read[0], 1), (bank_read[1], 1), (g_st[0], 16), (g_st[1], 16), (tile_done, 4),
                      (c_mm, 4), (c_ev, 4), (cf_ready, 4), (c_st, 64), (mod_step, 1), (mod_add, 1), (primed, 1)]
            for n, (counter, start) in enumerate(starts):
                nc.vector.memset(spare[:, n:n + 1], 0.0).then_inc(counter, start)
            dve.wait_ge(const_in, 64)
            steps = [0]

            def step(ins):
                steps[0] += 1
                ins.then_inc(rope_step, 1)
                dve.wait_ge(rope_step, steps[0])

            step(nc.vector.tensor_copy(ang[:], pos_i[:]))
            step(nc.vector.tensor_scalar(ang[:], ang[:], con[:, K_INV:K_INV + 1], None, ALU.mult))
            for k in range(2):
                if k == 1:
                    dve.wait_ge(rope_sin, 2)
                step(nc.vector.tensor_scalar(turn[:], ang[:], 1 / (2 * np.pi), 0.25 * k, ALU.mult, ALU.add))
                step(nc.vector.tensor_scalar(turn[:], turn[:], MAGIC, None, ALU.add))
                step(nc.vector.tensor_scalar(turns[:], turn[:], MAGIC, None, ALU.subtract))
                step(nc.vector.scalar_tensor_tensor(out=turn[:], in0=turns[:], scalar=-TP1, in1=ang[:],
                                                    op0=ALU.mult, op1=ALU.add))
                step(nc.vector.scalar_tensor_tensor(out=turn[:], in0=turns[:], scalar=-TP2, in1=turn[:],
                                                    op0=ALU.mult, op1=ALU.add))
                step(nc.vector.scalar_tensor_tensor(out=turn[:], in0=turns[:], scalar=-TP3, in1=turn[:],
                                                    op0=ALU.mult, op1=ALU.add))
                step(nc.vector.tensor_scalar(turn[:], turn[:], 0.5 * np.pi * k, None, ALU.add))
                nc.vector.tensor_scalar(turn[:], turn[:], PI, -PI, ALU.min, ALU.max).then_inc(rope_sin, 1)
            def modulate(row, total):
                nc.vector.tensor_tensor_reduce(out=row, in0=row, in1=cact[:], scale=1.0, scalar=0.0,
                                               op0=ALU.mult, op1=ALU.add, accum_out=total).then_inc(mod_step, 1)

            dve.wait_ge(c_silu, 1)
            for n in range(ADA_1):
                if n % 4 == 0:
                    dve.wait_ge(ada_in[n // 4], 64)
                modulate(rows0[:, n], mv[:, C + n:C + n + 1])

            with dve.Fori(0, DEPTH) as l:
                ll = dve.snap(l + 0)
                nc.vector.tensor_copy(lp[:], params[:, bass.ds(ll, 1)].rearrange("p o n -> p (o n)")).then_inc(lay, 1)
                dve.wait_ge(lay, 3 * l + 1)
                dve.wait_ge(mod_step, l * ADA_ALL + ADA_1 + 1)
                dve.wait_ge(mod_add, 3 * C // 4 * l + 1)
                nc.vector.tensor_tensor(md[:, 0:ADA_1], mv[:, C:3 * C], lp[:, O_AB:O_AB + ADA_1],
                                        ALU.add).then_inc(mod_sum, 1)
                dve.wait_ge(mod_sum, 3 * l + 1)
                nc.vector.scalar_tensor_tensor(out=gs[:, 0], in0=md[:, C:2 * C], scalar=1.0, in1=lp[:, 0:C],
                                               op0=ALU.add, op1=ALU.mult).then_inc(lay, 1)

                def norm(w):
                    n = 2 * l + w
                    dve.wait_ge(rt_done, n + 1)
                    nc.vector.reciprocal(rstd[:], rstd[:]).then_inc(rs_done, 1)
                    dve.wait_ge(rs_done, n + 1)
                    for c in range(C):
                        if c >= 2:
                            dve.wait_ge(hs_done, n * C + c - 1)
                        nc.vector.tensor_tensor(hx[:, c % 2], xT[:, c], rstd[:], ALU.mult).then_inc(hx_done, 1)

                def read_no(i):
                    return l * (NE // 2) + i // 2 + 2

                dve.wait_ge(x_in, 16)
                norm(0)

                def q_dst(k):
                    return qT[:, k] if k < I_K else kT[:, k - I_K, P:P + T]

                def q_norm(k):
                    dve.wait_ge(qrt, l * 10 + k + 1)
                    nc.vector.reciprocal(hs[:, k % 2], hs[:, k % 2]).then_inc(qrs, 1)
                    dve.wait_ge(qrs, l * 10 + k + 1)
                    gain = lp[:, O_QG:O_QG + 1] if k < I_K else lp[:, O_KG:O_KG + 1]
                    nc.vector.scalar_tensor_tensor(out=hx[:, k % 2], in0=q_dst(k), scalar=gain, in1=hs[:, k % 2],
                                                   op0=ALU.mult, op1=ALU.mult).then_inc(qn, 1)
                    dve.wait_ge(qn, l * 10 + k + 1)
                    nc.vector.tensor_tensor(q_dst(k), hx[:, k % 2], cosT[:], ALU.mult).then_inc(qcos, 1)

                def q_rot(k):
                    dve.wait_ge(rot, l * 10 + k + 1)
                    if k >= 2:
                        dve.wait_ge(qrope, l * 10 + k - 1)
                    nc.vector.tensor_tensor(sg[:, k % 2], ps[:, 6], sinT[:], ALU.mult).then_inc(qa, 1)
                    dve.wait_ge(qa, l * 10 + k + 1)
                    dve.wait_ge(qcos, l * 10 + k + 1)
                    nc.vector.tensor_tensor(q_dst(k), q_dst(k), sg[:, k % 2], ALU.add).then_inc(qrope, 1)

                def middle_rows(k0, k1):
                    for n in range(ADA_1 + k0, ADA_1 + k1):
                        dve.wait_ge(ada_in[n % 4], (l * (ADA_ALL // 4) + n // 4 + 1) * 16)
                        modulate(rows[n % 4][:], md[:, n:n + 1])

                dve.wait_ge(h_ready, 2 * l * C + C)
                for k in range(10):
                    q_norm(k)
                    if k >= 1:
                        q_rot(k - 1)
                    middle_rows(2 * k, 2 * k + 2)
                q_rot(9)
                for n in range(NB):
                    if n == 0:
                        dve.wait_ge(pad0, 3 * l + 3)
                    dve.wait_ge(v_tr, l * NB + n + 1)
                    nc.vector.tensor_copy(vn[:, n + 1], ps[:, 2, 0:2 * P]).then_inc(v_ev, 1)
                middle_rows(20, 3 * C)
                dve.wait_ge(mod_step, l * ADA_ALL + ADA_2 + 1)
                nc.vector.tensor_tensor(md[:, ADA_1:ADA_2], md[:, ADA_1:ADA_2], lp[:, O_AB + ADA_1:O_AB + ADA_2],
                                        ALU.add).then_inc(mod_sum, 1)
                dve.wait_ge(mod_sum, 3 * l + 2)
                nc.vector.scalar_tensor_tensor(out=gs[:, 1], in0=md[:, 4 * C:5 * C], scalar=1.0, in1=lp[:, C:2 * C],
                                               op0=ALU.add, op1=ALU.mult).then_inc(lay, 1)

                def gated(c):
                    dve.wait_ge(bank_read[0], read_no(I_GLU + 2 * c))
                    dve.wait_ge(tile_done, l * NT + I_GLU + 2 * c + 1 + 5)
                    nc.vector.tensor_tensor(uT[:, c, PAD:PAD + T], ps[:, 1], sg[:, c % 2],
                                            ALU.mult).then_inc(bank_read[1], 1)

                def tap(nth):
                    c, k = 2 * (nth // (2 * TAPS)) + nth % 2, nth // 2 % TAPS
                    weight = lp[:, O_CW + TAPS * c + k:O_CW + TAPS * c + k + 1]
                    if k == 0:
                        dve.wait_ge(bank_read[1], read_no(I_GLU + 2 * c + 1))
                        ins = nc.vector.tensor_scalar(yT[:, c], uT[:, c, 0:T], weight, lp[:, O_CB + c:O_CB + c + 1],
                                                      ALU.mult, ALU.add)
                    else:
                        dve.wait_ge(conv_step, l * C * TAPS + nth - 1)
                        ins = nc.vector.scalar_tensor_tensor(out=yT[:, c], in0=uT[:, c, k:k + T], scalar=weight,
                                                             in1=yT[:, c], op0=ALU.mult, op1=ALU.add)
                    ins.then_inc(conv_step, 1)

                def taps(u, part):
                    n0 = (u - 2) * EARLY_TAPS
                    for nth in range(n0 + part * EARLY_TAPS // 3, n0 + (part + 1) * EARLY_TAPS // 3):
                        if 0 <= nth < EARLY * TAPS:
                            tap(nth)

                def row_stats(u):
                    n, g = u // NKV, u % NKV
                    sc = scores_sb[u % 2]
                    mask = con[:, K_M0:K_M0 + 256] if n == 0 else con[:, K_M1:K_M1 + 256]
                    sink = lp[:, O_SK + g * R:O_SK + (g + 1) * R]
                    k = l * 16 + u + 1
                    dve.wait_ge(s_mm, k)
                    if u >= 2:
                        dve.wait_ge(p_tr, l * 32 + 2 * u - 2)
                    nc.vector.scalar_tensor_tensor(
                        out=sc[:], in0=ps[:, 2:4].rearrange("q b (r k) -> q (b r) k", r=2), scalar=HEAD ** -0.5,
                        in1=mask.rearrange("q (o k) -> q o k", o=1).broadcast_to([P, R, 256]),
                        op0=ALU.mult, op1=ALU.add).then_inc(s_msk, 1)
                    dve.wait_ge(s_msk, k)
                    nc.vector.tensor_reduce(st4[:, 0], sc[:], AX, ALU.max).then_inc(a_max, 1)
                    dve.wait_ge(a_max, 2 * (l * 16 + u) + 1)
                    nc.vector.tensor_tensor(st4[:, 5], st4[:, 0], sink, ALU.max).then_inc(a_max, 1)
                    dve.wait_ge(a_max, 2 * (l * 16 + u) + 2)
                    nc.vector.tensor_tensor(st4[:, 3], sink, st4[:, 5], ALU.subtract).then_inc(a_den, 1)
                    nc.vector.tensor_scalar(st4[:, 1], st4[:, 5], -1.0, None, ALU.mult).then_inc(a_neg, 1)

                def normalise(u):
                    sc = scores_sb[u % 2]
                    dve.wait_ge(a_exp, l * 16 + u + 1)
                    nc.vector.tensor_tensor(st4[:, 0], st4[:, 2], st4[:, 4], ALU.add).then_inc(a_den, 1)
                    dve.wait_ge(a_den, 3 * (l * 16 + u) + 2)
                    nc.vector.reciprocal(st4[:, 5], st4[:, 0]).then_inc(a_den, 1)
                    dve.wait_ge(a_den, 3 * (l * 16 + u) + 3)
                    nc.vector.tensor_tensor(
                        sc[:], sc[:], st4[:, 5].rearrange("q (r o) -> q r o", o=1).broadcast_to([P, R, 256]),
                        ALU.mult).then_inc(a_nrm, 1)

                def attended_low(u):
                    n, g = u // NKV, u % NKV
                    p, lo64 = g // 2, (g % 2) * HEAD
                    dve.wait_ge(o_hid, l * 16 + u + 1)
                    dst = (slice(lo64, lo64 + HEAD), slice(p * R, (p + 1) * R), slice(n * P, (n + 1) * P))
                    nc.vector.tensor_tensor(o_lo[dst], ps[lo64:lo64 + HEAD, 6].rearrange("f (r q) -> f r q", r=R),
                                            o_hi[dst].bitcast(F32), ALU.subtract).then_inc(o_lod, 1)

                gated(0)
                row_stats(0)
                normalise(0)
                for u in range(16):
                    taps(u, 0)
                    if u < 15:
                        row_stats(u + 1)
                    taps(u, 1)
                    if u < 15:
                        normalise(u + 1)
                    if u < GLU_LATE and u % 2 == 1:
                        gated((u + 2) // 2)
                    taps(u, 2)
                    attended_low(u)
                def attn_gated(r, s):
                    c = dve.snap(4 * r + s)
                    dve.wait_ge(bank_read[0], read_no(I_AG + 2 * s) + 4 * r)
                    dve.wait_ge(tile_done, l * NT + I_AG + 2 * s + 8 * r + 1 + 5)
                    nc.vector.tensor_tensor(qT[:, bass.ds(c, 1)].rearrange("p o t -> p (o t)"),
                                            ps[:, 1], sg[:, s % 2], ALU.mult).then_inc(bank_read[1], 1)

                with dve.Fori(0, (C - EARLY) // 2) as r:
                    for k in range(TAPS):
                        for s in range(2):
                            c = 2 * r + s + EARLY
                            src = uT[:, bass.ds(c, 1), k:k + T].rearrange("p o t -> p (o t)")
                            dst = yT[:, bass.ds(c, 1)].rearrange("p o t -> p (o t)")
                            tap = lp[:, bass.ds(O_CW + k + TAPS * c, 1)]
                            if k == 0:
                                dve.wait_ge(bank_read[1], read_no(I_AG - 1))
                                ins = nc.vector.tensor_scalar(dst, src, tap, lp[:, bass.ds(O_CB + c, 1)],
                                                              ALU.mult, ALU.add)
                            else:
                                dve.wait_ge(conv_step, (l * C + c - s) * TAPS + 2 * k - 1 + s)
                                ins = nc.vector.scalar_tensor_tensor(out=dst, in0=src, scalar=tap, in1=dst,
                                                                     op0=ALU.mult, op1=ALU.add)
                            ins.then_inc(conv_step, 1)
                        if k in (8, 16, 24, 30):
                            attn_gated(r, -(-k // 8) - 1)
                b0 = l * LN_STEPS
                dve.wait_ge(ln_mm, l * 2 * C + C)
                nc.vector.tensor_scalar(hx[:, 0], ps[:, 7], 1.0 / D, None, ALU.mult).then_inc(ln_step, 1)
                dve.wait_ge(ln_step, b0 + 1)
                for c in range(C):
                    nc.vector.tensor_tensor(yT[:, c], yT[:, c], hx[:, 0], ALU.subtract).then_inc(ln_step, 1)
                dve.wait_ge(ln_silu, l * (C + 1) + 1)
                nc.vector.reciprocal(rstd[:], rstd[:]).then_inc(ln_step, 1)
                dve.wait_ge(ln_step, b0 + C + 2)
                for c in range(C):
                    if c >= 2:
                        dve.wait_ge(ln_silu, l * (C + 1) + 1 + c - 1)
                    nc.vector.tensor_tensor(hx[:, c % 2], yT[:, c], rstd[:], ALU.mult).then_inc(ln_step, 1)
                for m in range(C):
                    if m < FIRST_GATES:
                        i = I_CG + FIRST_GATES + m
                        dve.wait_ge(tile_done, l * NT + i + 5)
                        dve.wait_ge(bank_read[m % 2], read_no(I_CG + m))
                        b, gate = m % 2, cgate[:, m]
                    else:
                        i = I_CG + 2 * m + 1
                        dve.wait_ge(bank_read[0], read_no(i - 1))
                        dve.wait_ge(tile_done, l * NT + i + 5)
                        b, gate = 1, sg[:, m % 2]
                    if m >= 2:
                        dve.wait_ge(mrg_lo, l * C + m - 1)
                    else:
                        dve.wait_ge(ln_silu, (l + 1) * (C + 1))
                    nc.vector.tensor_tensor(hx[:, m % 2], ps[:, b], gate, ALU.mult).then_inc(bank_read[b], 1)
                    dve.wait_ge(bank_read[b], read_no(i))
                    nc.vector.tensor_tensor(hx[:, m % 2], hx[:, m % 2], qT[:, m], ALU.add).then_inc(mrg, 1)

                with dve.Fori(0, 4) as r:
                    for s in range(2):
                        c = dve.snap(2 * r + s)
                        dve.wait_ge(tile_done, l * NT + I_OUT + 2 * r + s + 5)
                        xc = xT[:, bass.ds(c, 1)].rearrange("p o t -> p (o t)")
                        nc.vector.scalar_tensor_tensor(out=xc, in0=ps[:, s], scalar=md[:, bass.ds(2 * C + c, 1)],
                                                       in1=xc, op0=ALU.mult, op1=ALU.add).then_inc(bank_read[s], 1)
                norm(1)

                with dve.Fori(0, NB) as tt:
                    ttv = dve.snap(tt + 0)
                    tb = l * (NB * TOP_STEPS) + tt * TOP_STEPS
                    count = [0]

                    def mark(ins):
                        count[0] += 1
                        ins.then_inc(top_step, 1)

                    def settle():
                        dve.wait_ge(top_step, tb + count[0])

                    def guard():
                        mark(nc.vector.memset(spare[:, 0:1], 0.0))

                    dve.wait_ge(r_ev, l * 16 + 16)
                    mark(nc.vector.tensor_copy(s_w[:], S_all[:, bass.ds(ttv, 1)].rearrange("t o h n -> t (o h) n")))
                    settle()
                    guard()

                    def top16(vals, ids, src, n):
                        for r8 in range(2):
                            for h in range(n):
                                mark(nc.vector.max(vals[:, h, 8 * r8:8 * r8 + 8], src[:, h]))
                            settle()
                            guard()
                            for h in range(n):
                                mark(nc.vector.max_index(ids[:, h, 8 * r8:8 * r8 + 8], vals[:, h, 8 * r8:8 * r8 + 8],
                                                         src[:, h]))
                            if r8 == 0:
                                settle()
                                guard()
                                for h in range(n):
                                    mark(nc.vector.match_replace(src[:, h], vals[:, h, 0:8], src[:, h], LOWEST))
                                settle()
                                guard()

                    top16(v16, i16, s_w, 2 * RH)
                    v4 = v16[:].rearrange("t (h p) k -> t h p k", p=2)
                    mark(nc.vector.tensor_tensor(
                        cand[:].rearrange("t h (a b) -> t h a b", a=TOPK),
                        v4[:, :, 0].rearrange("t h (k o) -> t h k o", o=1).broadcast_to([P, RH, TOPK, TOPK]),
                        v4[:, :, 1].rearrange("t h (o k) -> t h o k", o=1).broadcast_to([P, RH, TOPK, TOPK]),
                        ALU.add))
                    settle()
                    guard()
                    top16(t16, p16, cand, RH)
                    settle()
                    mark(nc.vector.tensor_copy(esum[:, 0:1].rearrange("t o h -> t h o"), t16[:, :, 0:1]))
                    settle()
                    nc.vector.tensor_tensor(t16[:], t16[:], esum[:, 0].rearrange("t (h o) -> t h o", o=1)
                                            .broadcast_to([P, RH, TOPK]), ALU.subtract).then_inc(g_exp, 1)
                    pos = p16[:].rearrange("t h k -> t (h k)")
                    mark(nc.vector.tensor_scalar(ab[:, 0], pos, 4, None, ALU.logical_shift_right))
                    mark(nc.vector.tensor_scalar(ab[:, 1], pos, TOPK - 1, None, ALU.bitwise_and))
                    mark(nc.vector.tensor_copy(i16f[:], i16[:]))
                    settle()
                    mark(nc.vector.tensor_copy(abf[:], ab[:]))
                    settle()
                    for p in range(2):
                        mark(nc.vector.tensor_tensor(
                            eq[:], abf[:, p].rearrange("t (k o) -> t k o", o=1).broadcast_to([P, RH * TOPK, TOPK]),
                            con[:, K_IOTA:K_IOTA + TOPK].rearrange("t (o a) -> t o a", o=1)
                            .broadcast_to([P, RH * TOPK, TOPK]), ALU.is_equal))
                        settle()
                        i4 = i16f[:].rearrange("t (h p) a -> t h p a", p=2)[:, :, p]
                        e4 = eq[:].rearrange("t (h k) a -> t h k a", h=RH)
                        mark(nc.vector.tensor_tensor(
                            e4, e4, i4.rearrange("t h (o a) -> t h o a", o=1).broadcast_to([P, RH, TOPK, TOPK]),
                            ALU.mult))
                        settle()
                        mark(nc.vector.tensor_reduce(routed[:, p], eq[:], AX, ALU.add))
                        settle()
                    dve.wait_ge(g_exp, 2 * (l * NB + tt) + 2)
                    mark(nc.vector.tensor_reduce(esum[:, 1], t16[:], AX, ALU.add))
                    settle()
                    mark(nc.vector.reciprocal(esum[:, 0], esum[:, 1]))
                    settle()
                    nc.vector.tensor_tensor(routed[:, 2].rearrange("t (h k) -> t h k", h=RH), t16[:],
                                            esum[:, 0].rearrange("t (h o) -> t h o", o=1)
                                            .broadcast_to([P, RH, TOPK]), ALU.mult).then_inc(rt_ready, 1)
                    assert count[0] == TOP_STEPS, count[0]
                    tc = dve.snap(P * tt)
                    dve.wait_ge(rt_tr, l * NB + tt + 1)
                    nc.vector.tensor_copy(ijg[:, :, bass.ds(tc, P)],
                                          ps[:, 6, 0:3 * P].rearrange("k (c t) -> k c t", c=3)).then_inc(rt_ev, 1)
                with dve.Fori(0, T // 16) as r:
                    dve.wait_ge(rt_ev, l * NB + NB)
                    for q in range(4):
                        dve.wait_ge(c_mm, l * 128 + 4 * r + q + 1)
                        for k in range(4):
                            t = 16 * r + 4 * q + k
                            nc.vector.tensor_scalar(oneL[:, 4 * q + k], iota, ijg[:, 0, bass.ds(t, 1)], None,
                                                    ALU.is_equal)
                            ins = nc.vector.tensor_scalar(oneR[:, 4 * q + k], iota, ijg[:, 1, bass.ds(t, 1)],
                                                          ijg[:, 2, bass.ds(t, 1)], ALU.is_equal, ALU.mult)
                        ins.then_inc(lr_done, 1)

                def coefficients(r, rows_too):
                    for s in range(4):
                        j = l * NKEYS + 4 * r + s
                        dve.wait_ge(cf_ready, j + 3)
                        dve.wait_ge(cg_in[s], (l * (NKEYS // 4) + r) * 32 + 32)
                        nc.vector.tensor_tensor(coef[:, s % 2], cg[:, s, 0], cg[:, s, 1], ALU.mult).then_inc(cg_free, 1)
                        dve.wait_ge(tile_done, l * NT + I_W + 4 * r + s + 3)
                        dve.wait_ge(cg_free, l * (NKEYS + 4) + 4 * r + s + 5)
                        nc.vector.tensor_copy(cf_hi[:, s % 2], coef[:, s % 2]).then_inc(cf_hid, 1)
                        dve.wait_ge(cf_hid, j + 1)
                        nc.vector.tensor_tensor(cf_lo[:, s % 2], coef[:, s % 2], cf_hi[:, s % 2].bitcast(F32),
                                                ALU.subtract).then_inc(cf_ready, 1)
                        if rows_too:
                            dve.wait_ge(ada_in[s], (l * (ADA_ALL // 4) + r + ADA_2 // 4 + 1) * 16)
                            if s == 0:
                                dve.wait_ge(mod_add, 3 * C // 4 * l + r + 1)
                            modulate(rows[s][:], macc[:, s:s + 1])

                with dve.Fori(0, 3 * C // 4) as r:
                    coefficients(r, True)
                    col = dve.snap(4 * r)
                    dve.wait_ge(mod_step, l * ADA_ALL + ADA_2 + 4 * r + 5)
                    nc.vector.tensor_copy(mv[:, bass.ds(col, 4)], macc[:]).then_inc(mod_add, 1)
                with dve.Fori(3 * C // 4, NKEYS // 4) as r:
                    coefficients(r, False)
                dve.wait_ge(mod_add, 3 * C // 4 * (l + 1) + 1)
                nc.vector.tensor_tensor(md[:, ADA_2:ADA_ALL], mv[:, 0:C], lp[:, O_AB + ADA_2:O_AB + ADA_ALL],
                                        ALU.add).then_inc(mod_sum, 1)
                dve.wait_ge(mod_sum, 3 * l + 3)
                dve.wait_ge(tile_done, (l + 1) * NT + 4)
                for c in range(C):
                    nc.vector.scalar_tensor_tensor(out=xT[:, c], in0=ps[:, c], scalar=md[:, 5 * C + c:5 * C + c + 1],
                                                   in1=xT[:, c], op0=ALU.mult, op1=ALU.add).then_inc(x_upd, 1)
                dve.wait_ge(x_upd, (l + 1) * C)


_OUT = [((1, T, D), "float32")]


def lay_tiles(w):
    return w.reshape(C, P, -1, P).transpose(2, 1, 0, 3)


def kernel(**inputs):
    import concourse.bacc as bacc
    from concourse.bass_utils import run_bass_kernel_spmd as run

    a = {k: np.asarray(v) for k, v in inputs.items()}
    heads = [R * (2 * p + h) + r for p in range(2) for r in range(R) for h in range(2)]
    qcols = np.concatenate([np.arange(HEAD) + HEAD * h for h in heads])
    tiles = []
    for l in range(DEPTH):
        w = a["w_in"][l]
        q, k, v, ga, gb, g1, g2 = np.split(w, np.cumsum([D, 256, 256, D, D, D]), axis=1)
        pair = lambda x, y: np.stack([lay_tiles(x), lay_tiles(y)], 1).reshape(2 * C, P, C, P)
        conv, gate = lay_tiles(a["w_o_conv"][l]), lay_tiles(g2)
        f = FIRST_GATES
        tiles += [lay_tiles(q[:, qcols]), lay_tiles(k), lay_tiles(v), pair(gb, ga),
                  pair(g1, a["w_o_attn"][l][qcols]), gate[:f], conv[:f],
                  np.stack([gate[f:], conv[f:]], 1).reshape(-1, P, C, P), lay_tiles(a["w_out"][l]),
                  lay_tiles(a["peer_w_query"][l]),
                  a["peer_u"][l].reshape(P, NKEYS, C, P).transpose(1, 3, 2, 0),
                  a["peer_v"][l].reshape(P, NKEYS, C, P).transpose(1, 0, 2, 3)]
    stream = np.concatenate(tiles)
    chunked = lambda x: x.reshape(DEPTH, -1, P).transpose(2, 0, 1)
    rows = lambda x: np.broadcast_to(x[None], (P,) + x.shape)
    params = np.concatenate([
        chunked(a["norm_mix_g"]), chunked(a["norm_ffn_g"]),
        a["conv_w"].reshape(DEPTH, TAPS, C, P).transpose(3, 0, 2, 1).reshape(P, DEPTH, -1),
        chunked(a["conv_b"]), chunked(a["conv_ln_g"]), chunked(a["conv_ln_b"]),
        np.tile(a["q_norm_g"], (1, 2)).T[:, :, None], np.tile(a["k_norm_g"], (1, 2)).T[:, :, None],
        rows(a["attn_sinks"]), chunked(a["ada_b"])], axis=2)
    ada = a["ada_w"].transpose(0, 2, 1).reshape(DEPTH * ADA_ALL, P, C, P)
    arrays = {
        "stream": stream,
        "ada": np.concatenate([ada, ada[:ADA_1]]).reshape(-1, P, D),
        "params_in": params,
        "sub_keys": a["peer_sub_keys"].reshape(DEPTH, 2 * RH, NKEYS, P).transpose(0, 3, 1, 2),
        "constants": constants(),
        "x_in": a["x"][0].T.reshape(C, P, T).transpose(1, 0, 2),
        "c_in": a["c"],
        "pos_in": a["positions"],
    }
    arrays = {k: np.ascontiguousarray(v) for k, v in arrays.items()}
    nc = bacc.Bacc("TRN2", target_bir_lowering=False, num_devices=1)
    aps = [nc.dram_tensor(k, v.shape, mybir.dt.from_np(v.dtype), kind="ExternalInput").ap() for k, v in arrays.items()]
    c_scr = nc.dram_tensor("c_scratch", (NB, P, NKEYS, P), F32).ap()
    g_scr = nc.dram_tensor("gelu_scratch", (NKEYS, P, T), F32).ap()
    out = nc.dram_tensor("trunk_out", (P, C, T), F32, kind="ExternalOutput").ap()
    build_trunk(nc, *aps, c_scr, g_scr, out)
    r = run(nc, [arrays], core_ids=[0])
    y = r.results[0]["trunk_out"]
    return np.ascontiguousarray(y.transpose(1, 0, 2).reshape(D, T).T)[None]
```
